# Optimizing a Trainium2 kernel written in Bass

```python
import math
import jax, jax.numpy as jnp
from jax import lax
import numpy as np

D_MODEL = 1024
BATCH = 1
SEQ = 512
DEPTH = 2
DEC_BATCH = 8
DEC_SEQ = 8
PAST_LEN = 4096
PAGE_SIZE = 128

D_MIX = D_MODEL
D_HALF = D_MIX // 2
LRU_HEADS = 8
LRU_HEAD_DIM = D_HALF // LRU_HEADS
LRU_CONV = 4
RG_C = 8.0
SC_CONV = 3
FFN_CONV = 3
D_FF = 2816
N_IN = 5 * D_HALF
EPS = 1e-6

kernel_name = "hybrid_rglru_shortconv_convffn_step"

def rmsnorm(x, g):
    xf = x.astype(jnp.float32)
    y = xf * lax.rsqrt(jnp.mean(xf * xf, axis=-1, keepdims=True) + EPS)
    return (y * g.astype(jnp.float32)).astype(x.dtype)

def causal_conv(x, buf, w):
    K = w.shape[0]
    T = x.shape[1]
    xp = jnp.concatenate([buf.astype(x.dtype), x], axis=1)
    y = xp[:, 0:T] * w[0]
    for k in range(1, K):
        y = y + xp[:, k:k + T] * w[k]
    return y, xp[:, T:]

def block_diag(x, w, b):
    B_, T_, _ = x.shape
    xh = x.reshape(B_, T_, LRU_HEADS, LRU_HEAD_DIM)
    y = jnp.einsum('bthi,hij->bthj', xh, w).reshape(B_, T_, D_HALF)
    return y + b

def rglru(x, r, i, lam, h0):
    xf = x.astype(jnp.float32)
    rf = r.astype(jnp.float32)
    if_ = i.astype(jnp.float32)
    log_a = -RG_C * rf * jax.nn.softplus(-lam.astype(jnp.float32))
    a = jnp.exp(log_a)
    mult = jnp.sqrt(-jnp.expm1(2.0 * log_a))
    b = mult * (if_ * xf)
    b = b.at[:, 0].add(a[:, 0] * h0.astype(jnp.float32))

    def comb(left, right):
        a1, b1 = left
        a2, b2 = right
        return a1 * a2, a2 * b1 + b2

    _, h = lax.associative_scan(comb, (a, b), axis=1)
    return h.astype(x.dtype), h[:, -1].astype(h0.dtype)

def layer(x, c, st_h, st_lc, st_sc, st_fc,
          w_ada, b_ada, norm1_g, norm2_g, w_in, lru_conv_w, lru_conv_b,
          lru_wa, lru_ba, lru_wx, lru_bx, lru_lambda, sc_conv_w, w_out,
          ffn_w_up, ffn_conv_w, ffn_w_down):
    mod = (jax.nn.silu(c) @ w_ada + b_ada)[:, None, :]
    sh1, sc1, g1, sh2, sc2, g2 = jnp.split(mod, 6, axis=-1)

    hn = rmsnorm(x, norm1_g) * (1.0 + sc1) + sh1
    proj = hn @ w_in
    xl, gl, bs, cs, hs = jnp.split(proj, 5, axis=-1)
    xc, new_lc = causal_conv(xl, st_lc, lru_conv_w)
    xc = xc + lru_conv_b
    r = jax.nn.sigmoid(block_diag(xc, lru_wa, lru_ba))
    ig = jax.nn.sigmoid(block_diag(xc, lru_wx, lru_bx))
    h_seq, h_last = rglru(xc, r, ig, lru_lambda, st_h)
    lru_out = h_seq * jax.nn.gelu(gl)
    zc, new_sc = causal_conv(cs * hs, st_sc, sc_conv_w)
    sc_out = bs * zc
    mix = jnp.concatenate([lru_out, sc_out], axis=-1) @ w_out
    x = x + g1 * mix

    hn2 = rmsnorm(x, norm2_g) * (1.0 + sc2) + sh2
    u, v = jnp.split(hn2 @ ffn_w_up, 2, axis=-1)
    uc, new_fc = causal_conv(u, st_fc, ffn_conv_w)
    x = x + g2 * ((jax.nn.gelu(uc) * v) @ ffn_w_down)
    return x, h_last, new_lc, new_sc, new_fc

def run_trunk(x, c, st_h, st_lc, st_sc, st_fc, w_ada, b_ada, norm1_g, norm2_g,
              w_in, lru_conv_w, lru_conv_b, lru_wa, lru_ba, lru_wx, lru_bx,
              lru_lambda, sc_conv_w, w_out, ffn_w_up, ffn_conv_w, ffn_w_down,
              final_g):
    hs, lcs, scs, fcs = [], [], [], []
    for l in range(DEPTH):
        x, h, lc, sc, fc = layer(
            x, c, st_h[l], st_lc[l], st_sc[l], st_fc[l],
            w_ada[l], b_ada[l], norm1_g[l], norm2_g[l], w_in[l], lru_conv_w[l],
            lru_conv_b[l], lru_wa[l], lru_ba[l], lru_wx[l], lru_bx[l],
            lru_lambda[l], sc_conv_w[l], w_out[l], ffn_w_up[l], ffn_conv_w[l],
            ffn_w_down[l])
        hs.append(h); lcs.append(lc); scs.append(sc); fcs.append(fc)
    y = rmsnorm(x, final_g)
    return y, jnp.stack(hs), jnp.stack(lcs), jnp.stack(scs), jnp.stack(fcs)

def setup_inputs(seed: int = 0) -> dict:
    key = jax.random.key(seed)
    ks = iter(jax.random.split(key, 40))
    nrm = lambda shape, s: jax.random.normal(next(ks), shape, jnp.float32) * s
    d = {}
    d["x_prompt"] = nrm((BATCH, SEQ, D_MODEL), 1.0)
    d["x_sample"] = nrm((DEC_BATCH, DEC_SEQ, D_MODEL), 1.0)
    d["c_prompt"] = nrm((BATCH, D_MODEL), 1.0)
    d["c_sample"] = nrm((DEC_BATCH, D_MODEL), 1.0)
    d["state_lru_h"] = nrm((DEPTH, DEC_BATCH, D_HALF), 0.5)
    d["state_lru_conv"] = nrm((DEPTH, DEC_BATCH, LRU_CONV - 1, D_HALF), 0.5)
    d["state_sc_conv"] = nrm((DEPTH, DEC_BATCH, SC_CONV - 1, D_HALF), 0.5)
    d["state_ffn_conv"] = nrm((DEPTH, DEC_BATCH, FFN_CONV - 1, D_FF), 0.5)
    d["w_ada"] = nrm((DEPTH, D_MODEL, 6 * D_MODEL), 0.5 * D_MODEL ** -0.5)
    d["b_ada"] = nrm((DEPTH, 6 * D_MODEL), 0.01)
    d["norm1_g"] = 1.0 + nrm((DEPTH, D_MODEL), 0.01)
    d["norm2_g"] = 1.0 + nrm((DEPTH, D_MODEL), 0.01)
    d["w_in"] = nrm((DEPTH, D_MODEL, N_IN), D_MODEL ** -0.5)
    d["lru_conv_w"] = nrm((DEPTH, LRU_CONV, D_HALF), LRU_CONV ** -0.5)
    d["lru_conv_b"] = nrm((DEPTH, D_HALF), 0.01)
    d["lru_wa"] = nrm((DEPTH, LRU_HEADS, LRU_HEAD_DIM, LRU_HEAD_DIM), LRU_HEAD_DIM ** -0.5)
    d["lru_ba"] = nrm((DEPTH, D_HALF), 0.01)
    d["lru_wx"] = nrm((DEPTH, LRU_HEADS, LRU_HEAD_DIM, LRU_HEAD_DIM), LRU_HEAD_DIM ** -0.5)
    d["lru_bx"] = nrm((DEPTH, D_HALF), 0.01)
    u = jax.random.uniform(next(ks), (DEPTH, D_HALF), jnp.float32, 0.9, 0.999)
    a0 = u ** (1.0 / RG_C)
    d["lru_lambda"] = jnp.log(a0) - jnp.log1p(-a0)
    d["sc_conv_w"] = nrm((DEPTH, SC_CONV, D_HALF), SC_CONV ** -0.5)
    d["w_out"] = nrm((DEPTH, D_MIX, D_MODEL), D_MIX ** -0.5)
    d["ffn_w_up"] = nrm((DEPTH, D_MODEL, 2 * D_FF), D_MODEL ** -0.5)
    d["ffn_conv_w"] = nrm((DEPTH, FFN_CONV, D_FF), FFN_CONV ** -0.5)
    d["ffn_w_down"] = nrm((DEPTH, D_FF, D_MODEL), D_FF ** -0.5)
    d["final_g"] = 1.0 + nrm((D_MODEL,), 0.01)
    return d

def reference(x_prompt, x_sample, c_prompt, c_sample, state_lru_h, state_lru_conv,
              state_sc_conv, state_ffn_conv, w_ada, b_ada, norm1_g, norm2_g, w_in,
              lru_conv_w, lru_conv_b, lru_wa, lru_ba, lru_wx, lru_bx, lru_lambda,
              sc_conv_w, w_out, ffn_w_up, ffn_conv_w, ffn_w_down, final_g):
    dt = x_prompt.dtype
    p_h = jnp.zeros((DEPTH, BATCH, D_HALF), dt)
    p_lc = jnp.zeros((DEPTH, BATCH, LRU_CONV - 1, D_HALF), dt)
    p_sc = jnp.zeros((DEPTH, BATCH, SC_CONV - 1, D_HALF), dt)
    p_fc = jnp.zeros((DEPTH, BATCH, FFN_CONV - 1, D_FF), dt)
    y_prompt, nh_p, nlc_p, nsc_p, nfc_p = run_trunk(
        x_prompt, c_prompt, p_h, p_lc, p_sc, p_fc, w_ada, b_ada, norm1_g, norm2_g,
        w_in, lru_conv_w, lru_conv_b, lru_wa, lru_ba, lru_wx, lru_bx, lru_lambda,
        sc_conv_w, w_out, ffn_w_up, ffn_conv_w, ffn_w_down, final_g)
    y_sample, nh_s, nlc_s, nsc_s, nfc_s = run_trunk(
        x_sample, c_sample, state_lru_h, state_lru_conv, state_sc_conv,
        state_ffn_conv, w_ada, b_ada, norm1_g, norm2_g, w_in, lru_conv_w,
        lru_conv_b, lru_wa, lru_ba, lru_wx, lru_bx, lru_lambda, sc_conv_w, w_out,
        ffn_w_up, ffn_conv_w, ffn_w_down, final_g)
    return (y_prompt, y_sample, nh_p, nlc_p, nsc_p, nfc_p, nh_s, nlc_s, nsc_s, nfc_s)


_drawn_inputs = setup_inputs


def setup_inputs(seed=0):
    import zlib

    import numpy as np

    out = dict(_drawn_inputs(seed))
    spreads = {}
    factors = {'norm1_g': 3.772,
     'norm2_g': 26.719,
     'lru_ba': 43.319,
     'lru_bx': 30.467,
     'final_g': 31.062,
     'lru_conv_b': 4.554}
    for name, (base, spread) in spreads.items():
        noise = np.random.default_rng([zlib.crc32(name.encode()), seed]).standard_normal(out[name].shape)
        drawn = base * np.exp(spread * noise) if base else spread * noise
        out[name] = __import__('jax').numpy.asarray(drawn.astype(out[name].dtype))
    for name, factor in factors.items():
        out[name] = (out[name] * factor).astype(out[name].dtype)
    return out
```

```python
from contextlib import ExitStack

import concourse.bass as bass
from concourse import mybir

F32 = mybir.dt.float32
F32R = mybir.dt.float32r
ALU = mybir.AluOpType
ACT = mybir.ActivationFunctionType
P = 128
EPS = 1e-6
RG_C = 8.0


def hybrid_trunk_kernel(nc, a, o):
    L, D = a["w_ada"].shape[:2]
    SEQ = a["x_prompt"].shape[1]
    NB, TS = a["x_sample"].shape[:2]
    DH = a["lru_lambda"].shape[1]
    DFF = a["ffn_conv_w"].shape[2]
    HD = a["lru_wa"].shape[2]
    KX, KH, KF = D // P, DH // P, DFF // P
    HALF = (SEQ + NB * TS) // 2
    HP, HB = SEQ // 2, NB // 2
    HS = HALF - HP
    TOK = 2 * HALF
    PADS = 3
    SB0, SW = PADS + SEQ, PADS + TS
    PADW = SB0 + NB * SW
    NJ = 1 + NB
    GROUPS = [8, 8, KF - 16]
    NST_ = NB * TS
    assert (KX, KH, KF, HALF, NJ) == (8, 4, 22, 288, 9)

    V_BADA, V_N1, V_N2, V_CW, V_CB, V_BA, V_BX, V_LAM, V_SW = 0, 48, 56, 64, 80, 84, 88, 92, 96
    V_FW, V_SH, V_SLC, V_SSC, V_SF, V_SP, V_NSP, VN = 108, 174, 206, 302, 366, 718, 722, 726
    VT = [(0, 108, 4, 0), (1, 98, 4, 108), (2, 96, 4, 206), (3, 64, 4, 302),
          (4, 128, 5, 0), (5, 128, 5, 128), (6, 96, 5, 256)]
    N_LCS, N_SCS, N_HS, N_LCP, N_SCP, N_HP, N_FP, N_FS, NN = 0, 96, 160, 192, 204, 212, 216, 260, 612
    NST = [(0, 96), (96, 96), (192, 68), (260, 128), (388, 128), (516, 96)]
    NSO = [("lru_conv_s", 0, 0, 96, 0), ("sc_conv_s", 1, 0, 64, 0), ("lru_h_s", 1, 64, 32, 0),
           ("lru_conv_p", 2, 0, 12, 0), ("sc_conv_p", 2, 12, 8, 0), ("lru_h_p", 2, 20, 4, 0),
           ("ffn_conv_p", 2, 24, 44, 0), ("ffn_conv_s", 3, 0, 128, 0), ("ffn_conv_s", 4, 0, 128, 128),
           ("ffn_conv_s", 5, 0, 96, 256)]

    T_CS, T_HS, T_BS, T_GL, T_WOUT = 4, 8, 12, 16, 20
    T_UP, T_DN = [28, 52, 76], [44, 68, 88]
    TL, PL = 96, 48
    MOD_SH1, MOD_G1, MOD_SH2, MOD_SC2, MOD_G2 = 0, 16, 24, 32, 40
    MOD_SC1 = 8

    with ExitStack() as ctx:
        def sb(name, shape, dt=F32):
            return ctx.enter_context(nc.sbuf_tensor(name, shape, dt))

        def sem(name):
            return ctx.enter_context(nc.semaphore(name))

        X = sb("X", [P, KX, 2, HALF])
        NH = sb("norm_hi", [P, KX, 2, HALF], F32R)
        NL = sb("norm_lo", [P, KX, 2, HALF], F32R)
        MH = sb("mid_hi", [P, 8, 2, HALF], F32R)
        ML = sb("mid_lo", [P, 8, 2, HALF], F32R)
        RAW = sb("w_raw", [P, 2, 8, 256])
        WH = sb("w_hi", [P, 2, 8, 256], F32R)
        WL = sb("w_lo", [P, 2, 8, 256], F32R)
        AW = sb("ada_w", [P, 2048])
        CT = sb("silu_c", [P, KX, 32])
        VEC = sb("vec", [P, L, VN])
        CUR = sb("vec_now", [P, VN])
        MOD = sb("mod", [P, 6 * KX, NJ])
        GS = sb("gain", [P, KX, NJ])
        BNEXT = sb("bias_next", [P, 16])
        ADS = sb("ada_rows", [P, 512])
        BLK = sb("gate_w", [P, 2, KH, P])
        IDN = sb("ident", [P, P])
        ONE = sb("ones", [P, P])
        AVG = sb("avg", [P, 1])
        EPST = sb("eps", [P, 1])
        STD = sb("std", [P, 6])
        RST = sb("rstd", [P, 6])
        FG = sb("final_gain", [P, KX])
        NS = sb("new_states", [P, NN])
        SMALL = sb("small", [P, 160])
        XTMP = sb("x_tmp", [P, 2, NST_])
        WORK = sb("work", [P, 15 * PADW])

        def wk(i):
            return WORK[:, i * PADW:(i + 1) * PADW]

        CIN = [wk(0), wk(1)]
        XC = [wk(2 + c) for c in range(KH)]
        Z = [wk(6 + c) for c in range(KH)]
        TR, TI, TT = wk(10), wk(11), wk(12)
        HID = [wk(13), wk(14)]
        UC, GE = [wk(2), wk(3)], [wk(4), wk(5)]
        ACC = wk(14)[:, 0:TOK]
        SQ = [wk(11)[:, 0:TOK], wk(12)[:, 0:TOK]]
        T1 = wk(5)[:, 0:TOK]
        DIAG = WORK[:, 13 * PADW:13 * PADW + 6 * P].rearrange("p (i n) -> p i n", i=6)
        NSR = WORK[:, 7 * PADW:7 * PADW + 6 * P].rearrange("p (i n) -> p i n", i=6)
        XROW = WORK[:, 0:6 * D].rearrange("p (a n) -> p a n", a=6)
        VROW = WORK[:, 6 * D:6 * D + 15 * P].rearrange("p (a n) -> p a n", a=15)
        YROW = [RAW[:, i // 2].rearrange("p k n -> p (k n)")[:, (i % 2) * D:(i % 2 + 1) * D] for i in range(4)] \
            + [AW[:, 0:D], AW[:, D:2 * D]]

        PS = ctx.enter_context(nc.psum_tensor("ps", [P, 8, 512], F32))
        B_R, B_I, B_MISC, B_ADA = 4, 5, 6, 7

        def halves(t):
            return t[:, 0:TOK].rearrange("p (h n) -> p h n", h=2)

        def pr(t3):
            return t3[:, :, 0:HP]

        def sm(t3):
            return t3[:, :, HP:HALF].rearrange("p h (b t) -> p h b t", t=TS)

        def pp(t):
            return t[:, PADS:SB0].rearrange("p (h n) -> p h n", h=2)

        def spad(t):
            return t[:, SB0:PADW].rearrange("p (b n) -> p b n", b=NB)

        def sp4(t):
            return t[:, SB0:PADW].rearrange("p (h b n) -> p h b n", h=2, b=HB)[:, :, :, PADS:SW]

        def slot(s):
            return PS[:, 2 * s:2 * s + 2, 0:HALF]

        def perseq(v):
            return v.rearrange("p (h b u) -> p h b u", h=2, u=1).broadcast_to([P, 2, HB, TS])

        def token_tiles():
            return [(i, i // 2, (i % 2) * P, P) if i < 4 else (i, i - 4, HP, HS) for i in range(6)]

        tile_done = sem("tile_done")
        psum_free = [sem("psum_free0"), sem("psum_free1")]
        raw_full = [sem("raw_full0"), sem("raw_full1")]
        hi_done, lo_done = sem("hi_done"), sem("lo_done")
        ada_w_full, ada_slices = sem("ada_w_full"), sem("ada_slices")
        ada_rows_ready, ada_cols_done, mod_ready = sem("ada_rows_ready"), sem("ada_cols_done"), sem("mod_ready")
        blk_full, gate_done, gate_read, xc_ready = sem("blk_full"), sem("gate_done"), sem("gate_read"), sem("xc_ready")
        lru_act, m2_ready, scan_ready = sem("lru_act"), sem("m2_ready"), sem("scan_ready")
        conv_out, gelu_out = sem("conv_out"), sem("gelu_out")
        lru_prod, prod_hi, mid_ready = sem("lru_prod"), sem("prod_hi"), sem("mid_ready")
        norm_f, norm_hi, norm_ready = sem("norm_f"), sem("norm_hi_ready"), sem("norm_ready")
        x_ready, sq_ready, acc_ready = sem("x_ready"), sem("sq_ready"), sem("acc_ready")
        stat_done, std_ready, diag_ready, rs_done = sem("stat_done"), sem("std_ready"), sem("diag_ready"), sem("rs_done")
        ns_ready, ns_rows, ns_out = sem("ns_ready"), sem("ns_rows"), sem("ns_out")
        dve_step, act_step, pool_step = sem("dve_step"), sem("act_step"), sem("pool_step")
        c_in, v_in, x_in, ident_ready = sem("c_in"), sem("v_in"), sem("x_in"), sem("ident_ready")
        c_cols, c_sig, c_ready, v_cols, v_ready = sem("c_cols"), sem("c_sig"), sem("c_ready"), sem("v_cols"), sem("v_ready")
        x_cols, lam_e = sem("x_cols"), sem("lam_e")
        y_gain, y_cols, y_out = sem("y_gain"), sem("y_cols"), sem("y_out")
        y_rows = [sem("y_rows_act"), sem("y_rows_dve")]
        NVEC = 16 * L

        block = ctx.enter_context(nc.Block())

        def done(l, t):
            return l * TL + t + 5

        def read(l, t):
            return l * (TL // 2) + t // 2 + 2

        @block.sync
        def _(sp):
            for r, src in ((0, a["c_prompt"]), (8, a["c_sample"])):
                src = src.rearrange("b (k p) -> (b k) p", p=P)
                sp.dma_start(VROW[r:r + src.shape[0], 14, :], src).then_inc(c_in, 16)
            sp.dma_start(VROW[72:80, 14, :], a["final_g"].rearrange("(k p) -> k p", p=P)).then_inc(c_in, 16)
            sp.dma_start(XROW[:, 0:4, :], a["x_prompt"][0].rearrange("(a p) n -> p a n", p=P)).then_inc(x_in, 16)
            xs = a["x_sample"].rearrange("b t n -> (b t) n")
            for h in range(2):
                sp.dma_start(XROW[0:HS, 4 + h, :], xs[h * HS:(h + 1) * HS, :]).then_inc(x_in, 16)

            def load(p, s, src):
                src = src.rearrange("o (k p) c -> p (o k) c", p=P)
                sp.wait_ge(lo_done, p + 1)
                sp.dma_start(RAW[:, s, 0:src.shape[1], :], src).then_inc(raw_full[s], 16)

            with sp.Fori(0, L) as l:
                n = 0
                for c0 in (0, 3 * DH, 4 * DH, 2 * DH, DH):
                    for s in range(2):
                        load(l * PL + n, s, a["w_in"][bass.ds(l, 1), :, c0 + 256 * s:c0 + 256 * s + 256])
                        n += 1
                for j in range(4):
                    load(l * PL + n, j % 2, a["w_out"][bass.ds(l, 1), :, 256 * j:256 * j + 256])
                    n += 1
                for g, K in enumerate(GROUPS):
                    with sp.Fori(0, K // 2) as q:
                        for s in range(2):
                            load(l * PL + q * 2 + (n + s), s,
                                 a["ffn_w_up"][bass.ds(l, 1), :, bass.ds(q * 256 + (8 * g * P + s * DFF), 256)])
                    n += K
                    for j in range(4):
                        load(l * PL + n, j % 2,
                             a["ffn_w_down"][bass.ds(l, 1), 8 * g * P:(8 * g + K) * P, 256 * j:256 * j + 256])
                        n += 1
                assert n == PL
            ys = o["y_sample"].rearrange("b t n -> (b t) n")
            for i, h, t0, w in token_tiles():
                sp.wait_ge(y_rows[i % 2], i // 2 + 1)
                dst = o["y_prompt"][0, i * P:(i + 1) * P, :] if i < 4 else ys[h * HS:(h + 1) * HS, :]
                sp.dma_start(dst, YROW[i][0:w, :]).then_inc(y_out, 16)
            sp.wait_ge(y_out, 16 * 6)

        @block.gpsimd
        def _(pool):
            nc.gpsimd.memset(IDN[:], 0.0).then_inc(pool_step, 1)
            pool.wait_ge(pool_step, 1)
            nc.gpsimd.affine_select(out=IDN[:], in_=IDN[:], compare_op=ALU.not_equal, fill=1.0, base=0,
                                    pattern=[[-1, P]], channel_multiplier=1).then_inc(ident_ready, 1)
            nc.gpsimd.memset(ONE[:], 1.0).then_inc(ident_ready, 1)
            nc.gpsimd.memset(AVG[:], 1.0 / D).then_inc(ident_ready, 1)
            nc.gpsimd.memset(EPST[:], EPS).then_inc(ident_ready, 1)
            nc.gpsimd.memset(BLK[:], 0.0).then_inc(pool_step, 1)

            def ada_load(n, l, r, k):
                chunk = l * KX + k
                pool.wait_ge(ada_slices, n + 1)
                pool.dma_start(AW[:], a["w_ada"].rearrange("l (k p) c -> (l k) p c", p=P)
                               [bass.ds(chunk, 1), :, r * 2048:(r + 1) * 2048]
                               .rearrange("o p c -> p (o c)")).then_inc(ada_w_full, 16)

            with pool.Fori(0, KX) as k:
                ada_load(k, 0, 0, k)
            pool.wait_ge(pool_step, 2)
            with pool.Fori(0, L) as l:
                pool.wait_ge(gate_done, l * 8 + 1)
                for m, w in enumerate(("lru_wa", "lru_wx")):
                    for q in range(2):
                        src = a[w][bass.ds(l, 1)].rearrange("o (c q) i j -> q i (o c) j", q=2)[q]
                        pool.dma_start(BLK[q * HD:(q + 1) * HD, m, :, q * HD:(q + 1) * HD], src).then_inc(blk_full, 16)
                after = l * -1 + (L - 1)
                for i, (lr, r) in enumerate(((l, 1), (l, 2), (after, 0))):
                    with pool.Fori(0, KX) as k:
                        ada_load(l * 24 + k + (8 + 8 * i), lr, r, k)

        @block.tensor
        def _(pe):
            T = nc.tensor
            pe.sem_inc(tile_done, 4)
            pe.sem_inc(ada_slices, 1)
            pe.sem_inc(gate_done, 1)

            def tile(pair, i, xh, xl, order, ready=None):
                s, r, c = i % 2, i // 2, (i % 2) * P
                if i % 2 == 0:
                    pe.wait_ge(lo_done, pair + (r + 3))
                pe.wait_ge(psum_free[s], pair + (r + 1))
                for j, k in enumerate(order):
                    if ready is not None:
                        pe.wait_ge(ready[0], ready[1] + (j + 1))
                    for h in range(2):
                        out = PS[:, 2 * s + h, 0:HALF]
                        T.matmul(out, WH[:, r, k, c:c + P], xh[:, k, h, :], start=(j == 0), stop=False)
                        T.matmul(out, WH[:, r, k, c:c + P], xl[:, k, h, :], start=False, stop=False)
                        last = T.matmul(out, WL[:, r, k, c:c + P], xh[:, k, h, :], start=False,
                                        stop=(j == len(order) - 1))
                last.then_inc(tile_done, 1)

            def ada_slice(n, k):
                pe.wait_ge(ada_w_full, n * 16 + 16)
                for g in range(4):
                    last = T.matmul(PS[32 * g:32 * g + 32, B_ADA, :], CT[:, k, :], AW[:, g * 512:(g + 1) * 512],
                                    start=(k == 0), stop=(k == KX - 1))
                last.then_inc(ada_slices, 1)

            def ada_turn(m):
                pe.wait_ge(ada_rows_ready, m)
                for q in range(4):
                    last = T.transpose(PS[:, B_MISC, q * P:(q + 1) * P], ADS[:, q * P:(q + 1) * P], IDN[:])
                last.then_inc(ada_cols_done, 1)

            def norm_stats(m):
                pe.wait_ge(acc_ready, m)
                for i, h, t0, w in token_tiles():
                    last = T.matmul(PS[0:w, B_ADA, i:i + 1], ACC[:, h * HALF + t0:h * HALF + t0 + w], AVG[:],
                                    start=True, stop=True)
                last.then_inc(stat_done, 1)

            def norm_spread(m):
                pe.wait_ge(diag_ready, m)
                for i, h, t0, w in token_tiles():
                    last = T.matmul(PS[:, 4 + h, t0:t0 + w], ONE[0:w, :], DIAG[0:w, i, 0:w], start=True, stop=True)
                last.then_inc(rs_done, 1)

            pe.wait_ge(ident_ready, 4)
            pe.wait_ge(c_in, 48)
            T.transpose(PS[:, B_MISC, 0:80], VROW[0:80, 14, :], IDN[0:80, 0:80]).then_inc(c_cols, 1)
            pe.wait_ge(v_in, 16 * NVEC)
            for l in range(L):
                if l:
                    pe.wait_ge(v_ready, 2 * l)
                for i, n, b, c in VT:
                    last = T.transpose(PS[:, b, c:c + n], VROW[0:n, 7 * l + i, :], IDN[0:n, 0:n])
                last.then_inc(v_cols, 1)
            pe.wait_ge(x_in, 48)
            for k in range(KX):
                if k >= 2:
                    pe.wait_ge(x_ready, k - 1)
                for i, h, t0, w in token_tiles():
                    last = T.transpose(PS[:, 2 * (k % 2) + h, t0:t0 + w], XROW[0:w, i, k * P:(k + 1) * P], IDN[0:w, 0:w])
                last.then_inc(x_cols, 1)
            pe.wait_ge(c_ready, 1)
            for k in range(KX):
                ada_slice(k, k)
            ada_turn(1)

            with pe.Fori(0, L) as l:
                pe.wait_ge(ada_rows_ready, l * 3 + 1)
                norm_stats(l * 2 + 1)
                norm_spread(l * 2 + 1)
                for t in range(T_UP[0]):
                    if t < T_WOUT:
                        tile(l * PL + t // 4 * 2, t % 4, NH, NL, range(KX), (norm_ready, l * 16) if t == 0 else None)
                    else:
                        tile(l * PL + t // 4 * 2, t % 4, MH, ML, [4, 5, 6, 7, 0, 1, 2, 3],
                             (mid_ready, l * 30) if t == T_WOUT else None)
                    if t in (8, 20):
                        ada_turn(l * 3 + (2 if t == 8 else 3))
                    if not 8 <= t < 12:
                        i, k = (0, t) if t < 8 else (1, t - 12) if t < 20 else (2, t - 20)
                        if k == 0:
                            pe.wait_ge(ada_rows_ready, l * 3 + (i + 1))
                        ada_slice(l * 24 + (8 + 8 * i + k), k)
                    if t in (9, 11, 13, 15):
                        c = (t - 9) // 2
                        pe.wait_ge(xc_ready, l * 4 + (c + 1))
                        if c == 0:
                            pe.wait_ge(blk_full, l * 64 + 64)
                            pe.wait_ge(mod_ready, l * 3 + 2)
                        else:
                            pe.wait_ge(gate_read, l * 8 + 2 * c)
                        for m, b in ((0, B_R), (1, B_I)):
                            T.matmul(PS[:, b, :], BLK[:, m, c, :], XC[c][:, PADS:SB0], start=True, stop=True)
                            T.matmul(PS[:, B_MISC, m * NST_:(m + 1) * NST_], BLK[:, m, c, :],
                                     spad(XC[c])[:, :, PADS:SW], start=True, stop=True).then_inc(gate_done, 1)
                pe.wait_ge(ada_rows_ready, l * 3 + 4)
                norm_stats(l * 2 + 2)
                ada_turn(l * 3 + 4)
                norm_spread(l * 2 + 2)
                made = 8
                for g, K in enumerate(GROUPS):
                    with pe.Fori(0, K // 2) as q:
                        for i in range(4):
                            tile(l * PL + q * 2 + T_UP[g] // 2, i, NH, NL, range(KX),
                                 (norm_ready, l * 16 + 8) if g == 0 and i == 0 else None)
                    if g == 2:
                        pe.wait_ge(ns_ready, l + 1)
                        pe.wait_ge(mod_ready, l * 3 + 4)
                        for i, (c0, n) in enumerate(NST):
                            last = T.transpose(PS[0:n, B_MISC if i < 4 else B_R, (i % 4) * P:(i % 4 + 1) * P],
                                               NS[:, c0:c0 + n], IDN[:])
                        last.then_inc(ns_rows, 1)
                    with pe.Fori(0, 2) as q:
                        for i in range(4):
                            tile(l * PL + q * 2 + T_DN[g] // 2, i, MH, ML, range(K),
                                 (mid_ready, l * 30 + made) if i == 0 else None)
                    made += K
            norm_stats(2 * L + 1)
            for i, h, t0, w in token_tiles():
                s = i % 2
                if i >= 2:
                    pe.wait_ge(y_rows[s], i // 2)
                for k in range(KX):
                    if i == 0:
                        pe.wait_ge(y_gain, k + 1)
                    last = T.transpose(PS[0:w, 2 * s + k // 4, (k % 4) * P:(k % 4 + 1) * P], X[:, k, h, t0:t0 + w], IDN[:])
                last.then_inc(y_cols, 1)

        @block.scalar
        def _(act):
            A = nc.scalar.activation
            act.sem_inc(ns_out, 16)
            for l in range(L):
                def rows(name):
                    return a[name][l].rearrange("(k p) -> k p", p=P)
                fs = a["state_ffn_conv"][l].rearrange("b k (c p) -> (b k c) p", p=P)
                for i, r, src in (
                        (0, V_BADA, rows("b_ada")), (0, V_N1, rows("norm1_g")), (0, V_N2, rows("norm2_g")),
                        (0, V_CW, a["lru_conv_w"][l].rearrange("k (c p) -> (k c) p", p=P)),
                        (0, V_CB, rows("lru_conv_b")), (0, V_BA, rows("lru_ba")), (0, V_BX, rows("lru_bx")),
                        (0, V_LAM, rows("lru_lambda")),
                        (0, V_SW, a["sc_conv_w"][l].rearrange("k (c p) -> (k c) p", p=P)),
                        (1, 0, a["ffn_conv_w"][l].rearrange("k (c p) -> (k c) p", p=P)),
                        (1, V_SH - V_FW, a["state_lru_h"][l].rearrange("b (c p) -> (b c) p", p=P)),
                        (2, 0, a["state_lru_conv"][l].rearrange("b k (c p) -> (b k c) p", p=P)),
                        (3, 0, a["state_sc_conv"][l].rearrange("b k (c p) -> (b k c) p", p=P)),
                        (4, 0, fs[0:128]), (5, 0, fs[128:256]), (6, 0, fs[256:352])):
                    act.dma_start(VROW[r:r + src.shape[0], 7 * l + i, :], src).then_inc(v_in, 16)

            def split(l, n, q=0):
                s = n % 2
                act.wait_ge(raw_full[s], l * (8 * PL) + q * 16 + 16 * (n // 2 + 1))
                act.wait_ge(tile_done, l * TL + q * 4 + (2 * n + 2))
                A(WH[:, s], RAW[:, s], ACT.Copy).then_inc(hi_done, 1)

            def ada_rows(m, first=False):
                act.wait_ge(ada_slices, m * 8 + 1)
                if not first:
                    act.wait_ge(ada_cols_done, m - 1)
                A(ADS[:], PS[:, B_ADA, :], ACT.Copy).then_inc(ada_rows_ready, 1)

            def std(m):
                act.wait_ge(stat_done, m)
                A(STD[:, 0:4], PS[:, B_ADA, 0:4], ACT.Sqrt, bias=EPST[:])
                A(STD[0:HS, 4:6], PS[0:HS, B_ADA, 4:6], ACT.Sqrt, bias=EPST[0:HS, :]).then_inc(std_ready, 1)

            def norm_round(n):
                for k in range(KX):
                    act.wait_ge(norm_f, n + (k + 1))
                    A(NH[:, k], halves(HID[k % 2]), ACT.Copy).then_inc(norm_hi, 1)

            def square(n, m):
                act.wait_ge(x_ready, n + (m + 1))
                A(halves(SQ[m % 2]), X[:, m], ACT.Square).then_inc(sq_ready, 1)

            act.wait_ge(c_cols, 1)
            A(SMALL[:, 0:72], PS[:, B_MISC, 0:72], ACT.Sigmoid).then_inc(c_sig, 1)
            for l in range(L):
                act.wait_ge(v_cols, l + 1)
                A(VEC[:, l, 0:366], PS[:, 4, 0:366], ACT.Copy).then_inc(v_ready, 1)
                A(VEC[:, l, 366:718], PS[:, 5, 0:352], ACT.Copy).then_inc(v_ready, 1)
            act.wait_ge(v_ready, 2 * L)
            for l in range(L):
                A(SMALL[:, 80 + 4 * l:84 + 4 * l], VEC[:, l, V_LAM:V_LAM + 4], ACT.Abs).then_inc(act_step, 1)
            act.wait_ge(act_step, L)
            A(SMALL[:, 88:96], SMALL[:, 80:88], ACT.Exp, scale=-1.0).then_inc(lam_e, 1)
            for k in range(KX):
                square(0, k)
            ada_rows(1, first=True)

            with act.Fori(0, L) as l:
                split(l, 0)
                std(l * 2 + 1)
                norm_round(l * 16)
                split(l, 1)
                for c in range(KH):
                    act.wait_ge(tile_done, done(l, c))
                    if c >= 2:
                        act.wait_ge(xc_ready, l * 4 + (c - 1))
                    A(pp(CIN[c % 2]), pr(slot(c % 2)), ACT.Copy)
                    A(sp4(CIN[c % 2]), sm(slot(c % 2)), ACT.Copy).then_inc(psum_free[c % 2], 1)
                    if c == 1:
                        split(l, 2)
                split(l, 3)
                act.wait_ge(ns_out, l * (16 * len(NSO)) + 16)
                for c in range(KH):
                    act.wait_ge(tile_done, done(l, T_CS + c))
                    A(pp(Z[c]), pr(slot(c % 2)), ACT.Copy)
                    A(sp4(Z[c]), sm(slot(c % 2)), ACT.Copy).then_inc(psum_free[c % 2], 1)
                    if c == 1:
                        split(l, 4)
                ada_rows(l * 3 + 2)
                split(l, 5)

                def gates(c):
                    if c:
                        act.wait_ge(scan_ready, l * 4 + c)
                    act.wait_ge(gate_done, l * 8 + (2 * c + 3))
                    for m, (row, b, v) in enumerate(((TR, B_R, V_BA), (TI, B_I, V_BX))):
                        bias = CUR[:, v + c:v + c + 1]
                        A(row[:, PADS:SB0], PS[:, b, :], ACT.Sigmoid, bias=bias)
                        A(spad(row)[:, :, PADS:SW], PS[:, B_MISC, m * NST_:(m + 1) * NST_].rearrange("p (b t) -> p b t", t=TS),
                          ACT.Sigmoid, bias=bias).then_inc(gate_read, 1)
                    act.wait_ge(gate_read, l * 8 + (2 * c + 2))
                    A(TT[:, PADS:], TR[:, PADS:], ACT.Tanh, scale=CUR[:, V_SP + c:V_SP + c + 1])
                    A(TR[:, PADS:], TR[:, PADS:], ACT.Exp, scale=CUR[:, V_NSP + c:V_NSP + c + 1]).then_inc(lru_act, 1)
                    act.wait_ge(m2_ready, l * 4 + (c + 1))
                    A(TT[:, PADS:], TT[:, PADS:], ACT.Sqrt).then_inc(lru_act, 1)

                def sc_round(c):
                    act.wait_ge(psum_free[c % 2], read(l, T_BS + c))
                    A(MH[:, 4 + c], halves(HID[c % 2]), ACT.Copy).then_inc(prod_hi, 1)

                gates(0)
                split(l, 6)
                gates(1)
                split(l, 7)
                sc_round(0)
                sc_round(1)
                split(l, 8)
                gates(2)
                sc_round(2)
                sc_round(3)
                split(l, 9)
                gates(3)
                for c in range(KH):
                    act.wait_ge(tile_done, done(l, T_GL + c))
                    if c >= 2:
                        act.wait_ge(lru_prod, l * 4 + (c - 1))
                    A(CIN[c % 2][:, PADS:PADS + TOK].rearrange("p (h n) -> p h n", h=2), slot(c % 2),
                      ACT.Gelu_apprx_tanh).then_inc(psum_free[c % 2], 1)
                    if c == 1:
                        split(l, 10)
                    act.wait_ge(lru_prod, l * 4 + (c + 1))
                    A(MH[:, c], halves(HID[c % 2]), ACT.Copy).then_inc(prod_hi, 1)
                ada_rows(l * 3 + 3)
                split(l, 11)
                for m in range(KX):
                    if m == 7:
                        ada_rows(l * 3 + 4)
                    square(l * 16 + 8, m)
                    if m in (1, 3, 5):
                        split(l, 12 + m // 2)
                std(l * 2 + 2)
                norm_round(l * 16 + 8)
                made = 0
                for g, K in enumerate(GROUPS):
                    act.preload_act_table(ACT.Gelu_apprx_tanh)
                    with act.Fori(0, K // 2) as q:
                        split(l, T_UP[g] // 2 + 1, q)
                        for e in range(2):
                            act.wait_ge(tile_done, l * TL + q * 4 + (T_UP[g] + e + 5))
                            A(pp(CIN[e]), pr(slot(e)), ACT.Copy)
                            A(sp4(CIN[e]), sm(slot(e)), ACT.Copy).then_inc(psum_free[e], 1)
                        split(l, T_UP[g] // 2 + 2, q)
                        for e in range(2):
                            act.wait_ge(conv_out, l * KF + q * 2 + (made + e + 1))
                            A(GE[e][:, PADS:], UC[e][:, PADS:], ACT.Gelu_apprx_tanh).then_inc(gelu_out, 1)
                        for e in range(2):
                            act.wait_ge(psum_free[e], l * PL + q * 2 + (T_UP[g] // 2 + 3))
                            A(MH[:, bass.ds(q * 2 + e, 1)].rearrange("p o h n -> p (o h) n"), halves(HID[e]), ACT.Copy)\
                                .then_inc(prod_hi, 1)
                    nd = T_DN[g] // 2
                    split(l, nd + 1)
                    if g < 2:
                        for n in range(nd + 2, nd + 5):
                            split(l, n)
                    else:
                        act.wait_ge(ns_rows, l + 1)
                        for i, (c0, n) in enumerate(NST):
                            A(NSR[0:n, i, :], PS[0:n, B_MISC if i < 4 else B_R, (i % 4) * P:(i % 4 + 1) * P], ACT.Copy)\
                                .then_inc(act_step, 1)
                        act.wait_ge(act_step, l * 6 + (L + 6))
                        for name, i, r, n, r0 in NSO:
                            dst = o["new_" + name][bass.ds(l, 1)]
                            dst = dst.rearrange("o b (c p) -> (o b c) p", p=P) if len(dst.shape) == 3 else \
                                dst.rearrange("o b k (c p) -> (o b k c) p", p=P)
                            act.dma_start(dst[r0:r0 + n], NSR[r:r + n, i, :]).then_inc(ns_out, 16)
                        for m in range(KX):
                            square(l * 16 + 16, m)
                            if m in (1, 3):
                                split(l, nd + 2 + m // 2)
                    made += K
            std(2 * L + 1)
            for i, h, t0, w in token_tiles():
                if i % 2 == 0:
                    act.wait_ge(y_cols, i + 1)
                    act.wait_ge(diag_ready, 2 * L + 1)
                    A(YROW[i][0:w].rearrange("p (b n) -> p b n", b=2), PS[0:w, 0:2, :], ACT.Copy,
                      scale=RST[0:w, i:i + 1]).then_inc(y_rows[0], 1)
            act.wait_ge(ns_out, 16 * L * len(NSO) + 16)

        @block.vector
        def _(dve):
            V = nc.vector

            class Steps:
                base, n = 0, 0

                def __call__(self, ins):
                    ins.then_inc(dve_step, 1)
                    self.n += 1
                    dve.wait_ge(dve_step, self.base + self.n)

            step = Steps()
            dve.sem_inc(lo_done, 2)
            dve.sem_inc(psum_free[0], 1)
            dve.sem_inc(psum_free[1], 1)

            def split(l, n, q=0):
                s = n % 2
                dve.wait_ge(hi_done, l * PL + q * 2 + (n + 1))
                V.tensor_tensor(WL[:, s], RAW[:, s], WH[:, s].bitcast(F32), ALU.subtract).then_inc(lo_done, 1)

            def low(dst_lo, src, hi, signal):
                V.tensor_tensor(dst_lo, src, hi.bitcast(F32), ALU.subtract).then_inc(signal, 1)

            def product(row, g2, g4, src, signal):
                V.tensor_tensor(pr(halves(row)), g2, pr(src), ALU.mult)
                V.tensor_tensor(sm(halves(row)), g4, sm(src), ALU.mult).then_inc(signal, 1)

            def modulation(m, c0, bias):
                dve.wait_ge(ada_cols_done, m)
                out = MOD[:, c0:c0 + 16, :].rearrange("p (g q) j -> p g q j", g=4)
                src = PS[:, B_MISC, :].rearrange("p (q g j) -> p g q j", q=4, g=4)[:, :, :, 0:NJ]
                b = bias.rearrange("p (g q u) -> p g q u", g=4, u=1).broadcast_to([P, 4, 4, NJ])
                V.tensor_tensor(out, src, b, ALU.add).then_inc(mod_ready, 1)
                dve.wait_ge(mod_ready, m)

            def gains(c0, v):
                step(V.tensor_scalar(GS[:], MOD[:, c0:c0 + KX, :], 1.0, None, ALU.add))
                g = CUR[:, v:v + KX].rearrange("p (k u) -> p k u", u=1).broadcast_to([P, KX, NJ])
                step(V.tensor_tensor(GS[:], GS[:], g, ALU.mult))

            def sum_square(n, m):
                dve.wait_ge(sq_ready, n + (m + 1))
                if m == 0:
                    ins = V.tensor_copy(ACC, SQ[0])
                else:
                    ins = V.tensor_tensor(ACC, ACC, SQ[m % 2], ALU.add)
                if m < KX - 1:
                    step(ins)
                else:
                    ins.then_inc(acc_ready, 1)

            def rstd(m):
                dve.wait_ge(std_ready, m)
                step(V.reciprocal(RST[:], STD[:]))
                V.tensor_tensor(DIAG, IDN[:].rearrange("p (u n) -> p u n", u=1).broadcast_to([P, 6, P]),
                                RST[:].rearrange("p (i u) -> p i u", u=1).broadcast_to([P, 6, P]),
                                ALU.mult).then_inc(diag_ready, 1)

            def normalise(m, n, sh):
                def lows(k):
                    dve.wait_ge(norm_hi, n + (k + 1))
                    low(NL[:, k], halves(HID[k % 2]), NH[:, k], norm_ready)
                dve.wait_ge(rs_done, m)
                for k in range(KX):
                    f = halves(HID[k % 2])
                    step(V.tensor_tensor(halves(T1), X[:, k], PS[:, 4:6, 0:HALF], ALU.mult))
                    V.tensor_scalar(pr(f), pr(halves(T1)), GS[:, k, 0:1], MOD[:, sh + k, 0:1], ALU.mult, ALU.add)
                    step(V.tensor_tensor(sm(f), sm(halves(T1)), perseq(GS[:, k, 1:NJ]), ALU.mult))
                    V.tensor_tensor(sm(f), sm(f), perseq(MOD[:, sh + k, 1:NJ]), ALU.add).then_inc(norm_f, 1)
                    if k:
                        lows(k - 1)
                lows(KX - 1)

            def residual(wait, s, xm, mod, free, signal=None):
                dve.wait_ge(tile_done, wait)
                V.scalar_tensor_tensor(out=pr(xm), in0=pr(slot(s)), scalar=mod(0, 1), in1=pr(xm),
                                       op0=ALU.mult, op1=ALU.add)
                tmp = XTMP[:, s].rearrange("p (h b t) -> p h b t", h=2, t=TS)
                V.tensor_tensor(tmp, sm(slot(s)), perseq(mod(1, NJ)), ALU.mult).then_inc(psum_free[s], 1)
                dve.wait_ge(psum_free[s], free)
                ins = V.tensor_tensor(sm(xm), sm(xm), tmp, ALU.add)
                if signal is None:
                    step(ins)
                else:
                    ins.then_inc(signal, 1)

            def conv3(out, row, w):
                step(V.tensor_scalar(out[:, PADS:], row[:, PADS:], w(2), None, ALU.mult))
                for k in range(2):
                    ins = V.scalar_tensor_tensor(out=out[:, PADS:], in0=row[:, k + 1:PADW - 2 + k], scalar=w(k),
                                                 in1=out[:, PADS:], op0=ALU.mult, op1=ALU.add)
                    if k == 0:
                        step(ins)
                return ins

            step(V.memset(CT[:], 0.0))
            step(V.memset(STD[:], 1.0))
            dve.wait_ge(c_sig, 1)
            step(V.tensor_tensor(CT[:, :, 0], PS[:, B_MISC, 0:8], SMALL[:, 0:8], ALU.mult))
            step(V.tensor_tensor(CT[:, :, 1:NJ], PS[:, B_MISC, 8:72].rearrange("p (b k) -> p k b", k=KX),
                                 SMALL[:, 8:72].rearrange("p (b k) -> p k b", k=KX), ALU.mult))
            V.tensor_copy(FG[:], PS[:, B_MISC, 72:80]).then_inc(c_ready, 1)
            for k in range(KX):
                dve.wait_ge(x_cols, k + 1)
                V.tensor_copy(X[:, k], slot(k % 2)).then_inc(x_ready, 1)
                if k:
                    sum_square(0, k - 1)
            sum_square(0, KX - 1)
            for row in CIN + [TR, TI]:
                step(V.memset(row[:, 0:PADS], 0.0))
            for row in Z + [TR, TI]:
                step(V.memset(spad(row)[:, :, 0:PADS], 0.0))
            dve.wait_ge(lam_e, 1)
            E, Zs, Z2, Q, M0 = (SMALL[:, c:c + 8] for c in (88, 96, 104, 112, 120))
            step(V.tensor_scalar(Q, E, 2.0, None, ALU.add))
            step(V.reciprocal(Q, Q))
            step(V.tensor_tensor(Zs, E, Q, ALU.mult))
            step(V.tensor_tensor(Z2, Zs, Zs, ALU.mult))
            step(V.tensor_scalar(Q, Z2, 1.0 / 17, None, ALU.mult))
            for d in (15, 13, 11, 9, 7, 5, 3):
                step(V.scalar_tensor_tensor(out=Q, in0=Q, scalar=1.0 / d, in1=Z2, op0=ALU.add, op1=ALU.mult))
            step(V.scalar_tensor_tensor(out=Q, in0=Q, scalar=1.0, in1=Zs, op0=ALU.add, op1=ALU.mult))
            for l in range(L):
                m0, q0 = M0[:, 4 * l:4 * l + 4], Q[:, 4 * l:4 * l + 4]
                step(V.tensor_scalar(m0, VEC[:, l, V_LAM:V_LAM + 4], -1.0, 0.0, ALU.mult, ALU.max))
                step(V.scalar_tensor_tensor(out=m0, in0=q0, scalar=2.0, in1=m0, op0=ALU.mult, op1=ALU.add))
                step(V.tensor_scalar(VEC[:, l, V_SP:V_SP + 4], m0, RG_C, None, ALU.mult))
                step(V.tensor_scalar(VEC[:, l, V_NSP:V_NSP + 4], m0, -RG_C, None, ALU.mult))
            modulation(1, MOD_SH1, VEC[:, 0, 0:16])
            before = step.n

            with dve.Fori(0, L) as l:
                step.base, step.n = l * DVE_STEPS + before, 0
                after = l * -1 + (L - 1)
                step(V.tensor_copy(CUR[:], VEC[:, bass.ds(l, 1), :].rearrange("p o n -> p (o n)")))
                gains(MOD_SC1, V_N1)
                split(l, 0)
                rstd(l * 2 + 1)
                normalise(l * 2 + 1, l * 16, MOD_SH1)
                split(l, 1)
                slc = CUR[:, V_SLC:V_SLC + 96].rearrange("p (b k c) -> p b k c", k=3, c=KH)
                nlcs = NS[:, N_LCS:N_LCS + 96].rearrange("p (b k c) -> p b k c", k=3, c=KH)
                nlcp = NS[:, N_LCP:N_LCP + 12].rearrange("p (k c) -> p k c", c=KH)
                for c in range(KH):
                    row, s = CIN[c % 2], c % 2
                    step(V.tensor_copy(spad(row)[:, :, 0:3], slc[:, :, :, c]))
                    dve.wait_ge(psum_free[s], read(l, c))
                    V.tensor_copy(nlcp[:, :, c], row[:, SB0 - 3:SB0])
                    V.tensor_copy(nlcs[:, :, :, c], spad(row)[:, :, SW - 3:SW])
                    cw = [CUR[:, V_CW + 4 * k + c:V_CW + 4 * k + c + 1] for k in range(4)]
                    out = XC[c][:, PADS:]
                    step(V.tensor_scalar(out, row[:, PADS:], cw[3], CUR[:, V_CB + c:V_CB + c + 1], ALU.mult, ALU.add))
                    for k in range(3):
                        ins = V.scalar_tensor_tensor(out=out, in0=row[:, k:PADW - 3 + k], scalar=cw[k], in1=out,
                                                     op0=ALU.mult, op1=ALU.add)
                        if k < 2:
                            step(ins)
                    ins.then_inc(xc_ready, 1)
                    if c == 1:
                        split(l, 2)
                split(l, 3)
                dve.wait_ge(ns_out, l * (16 * len(NSO)) + 16)
                ssc = CUR[:, V_SSC:V_SSC + 64].rearrange("p (b k c) -> p b k c", k=2, c=KH)
                for c in range(KH):
                    step(V.memset(Z[c][:, 0:PADS], 0.0))
                    step(V.tensor_copy(spad(Z[c])[:, :, 1:3], ssc[:, :, :, c]))
                split(l, 4)
                split(l, 5)

                def c_times_h(c):
                    s = c % 2
                    dve.wait_ge(psum_free[s], read(l, T_CS + c))
                    dve.wait_ge(tile_done, done(l, T_HS + c))
                    V.tensor_tensor(pp(Z[c]), pp(Z[c]), pr(slot(s)), ALU.mult)
                    V.tensor_tensor(sp4(Z[c]), sp4(Z[c]), sm(slot(s)), ALU.mult).then_inc(psum_free[s], 1)
                    dve.wait_ge(psum_free[s], read(l, T_HS + c))
                    V.tensor_copy(NS[:, N_SCP:N_SCP + 8].rearrange("p (k c) -> p k c", c=KH)[:, :, c], Z[c][:, SB0 - 2:SB0])
                    V.tensor_copy(NS[:, N_SCS:N_SCS + 64].rearrange("p (b k c) -> p b k c", k=2, c=KH)[:, :, :, c],
                                  spad(Z[c])[:, :, SW - 2:SW])

                def lru_m2(c):
                    dve.wait_ge(lru_act, l * 8 + (2 * c + 1))
                    step(V.tensor_tensor(CIN[1][:, PADS:], TR[:, PADS:], TR[:, PADS:], ALU.mult))
                    V.scalar_tensor_tensor(out=TT[:, PADS:], in0=CIN[1][:, PADS:], scalar=1.0, in1=TT[:, PADS:],
                                           op0=ALU.add, op1=ALU.mult).then_inc(m2_ready, 1)
                    step(V.tensor_tensor(TI[:, PADS:], TI[:, PADS:], XC[c][:, PADS:], ALU.mult))

                def lru_scan(c):
                    dve.wait_ge(lru_act, l * 8 + (2 * c + 2))
                    step(V.tensor_tensor(TI[:, PADS:], TI[:, PADS:], TT[:, PADS:], ALU.mult))
                    step(V.memset(spad(TI)[:, :, 0:2], 0.0))
                    h0 = CUR[:, V_SH:V_SH + 32].rearrange("p (b c) -> p b c", c=KH)
                    step(V.tensor_copy(spad(TI)[:, :, 2], h0[:, :, c]))
                    step(V.memset(spad(TR)[:, :, 0:PADS], 0.0))
                    V.tensor_tensor_scan(XC[c][:, PADS:], TR[:, PADS:], TI[:, PADS:], 0.0, ALU.mult, ALU.add)\
                        .then_inc(scan_ready, 1)
                    dve.wait_ge(scan_ready, l * 4 + (c + 1))
                    V.tensor_copy(NS[:, N_HP + c:N_HP + c + 1], XC[c][:, SB0 - 1:SB0])
                    V.tensor_copy(NS[:, N_HS:N_HS + 32].rearrange("p (b c) -> p b c", c=KH)[:, :, c],
                                  spad(XC[c])[:, :, SW - 1])

                def short_conv(c):
                    s = c % 2
                    step(conv3(CIN[0], Z[c], lambda k: CUR[:, V_SW + 4 * k + c:V_SW + 4 * k + c + 1]))
                    dve.wait_ge(tile_done, done(l, T_BS + c))
                    product(HID[s], pp(CIN[0]), sp4(CIN[0]), slot(s), psum_free[s])
                    dve.wait_ge(prod_hi, l * 30 + (c + 1))
                    low(ML[:, 4 + c], halves(HID[s]), MH[:, 4 + c], mid_ready)

                c_times_h(0)
                modulation(l * 3 + 2, 16, CUR[:, 16:32])
                c_times_h(1)
                lru_m2(0)
                c_times_h(2)
                lru_scan(0)
                split(l, 6)
                c_times_h(3)
                lru_m2(1)
                lru_scan(1)
                split(l, 7)
                short_conv(0)
                short_conv(1)
                split(l, 8)
                lru_m2(2)
                lru_scan(2)
                short_conv(2)
                short_conv(3)
                split(l, 9)
                lru_m2(3)
                lru_scan(3)
                for c in range(KH):
                    s = c % 2
                    dve.wait_ge(psum_free[s], read(l, T_GL + c))
                    gl = CIN[s][:, PADS:PADS + TOK].rearrange("p (h n) -> p h n", h=2)
                    product(HID[s], pp(XC[c]), sp4(XC[c]), gl, lru_prod)
                    if c == 1:
                        split(l, 10)
                    dve.wait_ge(prod_hi, l * 30 + (c + 5))
                    low(ML[:, c], halves(HID[s]), MH[:, c], mid_ready)
                split(l, 11)
                for m in range(KX):
                    residual(done(l, T_WOUT + m), m % 2, X[:, m], lambda a_, b_, m=m: MOD[:, MOD_G1 + m, a_:b_],
                             read(l, T_WOUT + m), x_ready)
                    if m == 0:
                        modulation(l * 3 + 3, 32, CUR[:, 32:48])
                        gains(MOD_SC2, V_N2)
                    else:
                        sum_square(l * 16 + 8, m - 1)
                    if m in (1, 3, 5):
                        split(l, 12 + m // 2)
                sum_square(l * 16 + 8, KX - 1)
                step(V.tensor_copy(BNEXT[:], VEC[:, bass.ds(after, 1), 0:16].rearrange("p o n -> p (o n)")))
                rstd(l * 2 + 2)
                modulation(l * 3 + 4, MOD_SH1, BNEXT[:])
                normalise(l * 2 + 2, l * 16 + 8, MOD_SH2)

                ssf = CUR[:, V_SF:V_SF + 352].rearrange("p (b k m) -> p b k m", k=2, m=KF)
                nfs = NS[:, N_FS:N_FS + 352].rearrange("p (b k m) -> p b k m", k=2, m=KF)
                nfp = NS[:, N_FP:N_FP + 44].rearrange("p (k m) -> p k m", m=KF)
                made = 0
                for g, K in enumerate(GROUPS):
                    base, at = step.base, step.n
                    with dve.Fori(0, K // 2) as q:
                        step.base, step.n = base + at + q * UP_STEPS, 0
                        split(l, T_UP[g] // 2 + 1, q)
                        for e in range(2):
                            row = CIN[e]
                            ch = bass.ds(q * 2 + (made + e), 1)
                            step(V.tensor_copy(spad(row)[:, :, 1:3], ssf[:, :, :, ch].rearrange("p b k o -> p b (k o)")))
                            dve.wait_ge(psum_free[e], l * PL + q * 2 + (T_UP[g] // 2 + 2))
                            V.tensor_copy(nfp[:, :, ch].rearrange("p k o -> p (k o)"), row[:, SB0 - 2:SB0])
                            V.tensor_copy(nfs[:, :, :, ch].rearrange("p b k o -> p b (k o)"), spad(row)[:, :, SW - 2:SW])
                            conv3(UC[e], row, lambda k: CUR[:, bass.ds(q * 2 + (V_FW + KF * k + made + e), 1)])\
                                .then_inc(conv_out, 1)
                        split(l, T_UP[g] // 2 + 2, q)
                        for e in range(2):
                            dve.wait_ge(tile_done, l * TL + q * 4 + (T_UP[g] + 2 + e + 5))
                            dve.wait_ge(gelu_out, l * KF + q * 2 + (made + e + 1))
                            product(HID[e], pp(GE[e]), sp4(GE[e]), slot(e), psum_free[e])
                            dve.wait_ge(prod_hi, l * 30 + q * 2 + (8 + made + e + 1))
                            mid = bass.ds(q * 2 + e, 1)
                            low(ML[:, mid].rearrange("p o h n -> p (o h) n"), halves(HID[e]),
                                MH[:, mid].rearrange("p o h n -> p (o h) n"), mid_ready)
                        assert step.n == UP_STEPS, step.n
                    step.base, step.n = base, at + UP_STEPS * (K // 2)
                    nd = T_DN[g] // 2
                    if g < 2:
                        base, at = step.base, step.n
                        with dve.Fori(0, 2) as q:
                            step.base, step.n = base + at + q * 4, 0
                            for e in range(4):
                                if e % 2 == 0:
                                    split(l, nd + 1 + e // 2, q)
                                residual(l * TL + q * 4 + (T_DN[g] + e + 5), e % 2,
                                         X[:, bass.ds(q * 4 + e, 1)].rearrange("p o h n -> p (o h) n"),
                                         lambda a_, b_, e=e: MOD[:, bass.ds(q * 4 + (MOD_G2 + e), 1), a_:b_]
                                         .rearrange("p o j -> p (o j)"),
                                         l * PL + q * 2 + (T_DN[g] // 2 + e // 2 + 2))
                            assert step.n == 4
                        step.base, step.n = base, at + 8
                    else:
                        V.tensor_copy(XTMP[:, 0, 0:1], NS[:, 0:1]).then_inc(ns_ready, 1)
                        split(l, nd + 1)
                        for m in range(KX):
                            residual(done(l, T_DN[g] + m), m % 2, X[:, m], lambda a_, b_, m=m: MOD[:, MOD_G2 + m, a_:b_],
                                     read(l, T_DN[g] + m), x_ready)
                            if m:
                                sum_square(l * 16 + 16, m - 1)
                            if m in (1, 3):
                                split(l, nd + 2 + m // 2)
                        sum_square(l * 16 + 16, KX - 1)
                    made += K
                assert step.n == DVE_STEPS, step.n
            step.base, step.n = L * DVE_STEPS + before, 0
            for k in range(KX):
                V.tensor_scalar(X[:, k], X[:, k], FG[:, k:k + 1], None, ALU.mult).then_inc(y_gain, 1)
            dve.wait_ge(std_ready, 2 * L + 1)
            V.reciprocal(RST[:], STD[:]).then_inc(diag_ready, 1)
            dve.wait_ge(diag_ready, 2 * L + 1)
            for i, h, t0, w in token_tiles():
                if i % 2:
                    dve.wait_ge(y_cols, i + 1)
                    V.tensor_scalar(YROW[i][0:w].rearrange("p (b n) -> p b n", b=2), PS[0:w, 2:4, :],
                                    RST[0:w, i:i + 1], None, ALU.mult).then_inc(y_rows[1], 1)


UP_STEPS = 6
DVE_STEPS = 196

_OUT = ["y_prompt", "y_sample", "new_lru_h_p", "new_lru_conv_p", "new_sc_conv_p", "new_ffn_conv_p",
        "new_lru_h_s", "new_lru_conv_s", "new_sc_conv_s", "new_ffn_conv_s"]
_INS = ["x_prompt", "x_sample", "c_prompt", "c_sample", "state_lru_h", "state_lru_conv", "state_sc_conv",
        "state_ffn_conv", "w_ada", "b_ada", "norm1_g", "norm2_g", "w_in", "lru_conv_w", "lru_conv_b", "lru_wa",
        "lru_ba", "lru_wx", "lru_bx", "lru_lambda", "sc_conv_w", "w_out", "ffn_w_up", "ffn_conv_w", "ffn_w_down",
        "final_g"]


def kernel(**inputs):
    import numpy as np
    import concourse.bacc as bacc
    from concourse.bass_utils import run_bass_kernel_spmd

    nc = bacc.Bacc("TRN2", target_bir_lowering=False, num_devices=1)
    arrays, a, o = {}, {}, {}
    for name in _INS:
        arrays["in_" + name] = x = np.ascontiguousarray(inputs[name])
        a[name] = nc.dram_tensor("in_" + name, x.shape, mybir.dt.from_np(x.dtype), kind="ExternalInput").ap()
    L, DB, _, DH = inputs["state_lru_conv"].shape
    DFF = inputs["state_ffn_conv"].shape[3]
    shapes = [inputs["x_prompt"].shape, inputs["x_sample"].shape]
    for b in (1, DB):
        shapes += [(L, b, DH), (L, b, 3, DH), (L, b, 2, DH), (L, b, 2, DFF)]
    for name, shape in zip(_OUT, shapes):
        o[name] = nc.dram_tensor("out_" + name, tuple(shape), F32, kind="ExternalOutput").ap()
    hybrid_trunk_kernel(nc, a, o)
    r = run_bass_kernel_spmd(nc, [arrays], core_ids=[0])
    return tuple(r.results[0]["out_" + name] for name in _OUT)
```

```python
from contextlib import ExitStack

import concourse.bass as bass
from concourse import mybir

F32 = mybir.dt.float32
F32R = mybir.dt.float32r
ALU = mybir.AluOpType
ACT = mybir.ActivationFunctionType
P = 128
EPS = 1e-6
RG_C = 8.0


def hybrid_trunk_kernel(nc, a, o):
    L, D = a["w_ada"].shape[:2]
    SEQ = a["x_prompt"].shape[1]
    NB, TS = a["x_sample"].shape[:2]
    DH = a["lru_lambda"].shape[1]
    DFF = a["ffn_conv_w"].shape[2]
    HD = a["lru_wa"].shape[2]
    KX, KH, KF = D // P, DH // P, DFF // P
    HALF = (SEQ + NB * TS) // 2
    HP, HB = SEQ // 2, NB // 2
    HS = HALF - HP
    TOK = 2 * HALF
    PADS = 3
    SB0, SW = PADS + SEQ, PADS + TS
    PADW = SB0 + NB * SW
    NJ = 1 + NB
    GROUPS = [8, 8, KF - 16]
    NST_ = NB * TS
    assert (KX, KH, KF, HALF, NJ) == (8, 4, 22, 288, 9)

    V_BADA, V_N1, V_N2, V_CW, V_CB, V_BA, V_BX, V_LAM, V_SW = 0, 48, 56, 64, 80, 84, 88, 92, 96
    V_FW, V_SH, V_SLC, V_SSC, V_SF, V_SP, V_NSP, VN = 108, 174, 206, 302, 366, 718, 722, 726
    VT = [(0, 108, 4, 0), (1, 98, 4, 108), (2, 96, 4, 206), (3, 64, 4, 302),
          (4, 128, 5, 0), (5, 128, 5, 128), (6, 96, 5, 256)]
    N_LCS, N_SCS, N_HS, N_LCP, N_SCP, N_HP, N_FP, N_FS, NN = 0, 96, 160, 192, 204, 212, 216, 260, 612
    NST = [(0, 96), (96, 96), (192, 68), (260, 128), (388, 128), (516, 96)]
    NSO = [("lru_conv_s", 0, 0, 96, 0), ("sc_conv_s", 1, 0, 64, 0), ("lru_h_s", 1, 64, 32, 0),
           ("lru_conv_p", 2, 0, 12, 0), ("sc_conv_p", 2, 12, 8, 0), ("lru_h_p", 2, 20, 4, 0),
           ("ffn_conv_p", 2, 24, 44, 0), ("ffn_conv_s", 3, 0, 128, 0), ("ffn_conv_s", 4, 0, 128, 128),
           ("ffn_conv_s", 5, 0, 96, 256)]

    T_CS, T_HS, T_BS, T_GL, T_WOUT = 4, 8, 12, 16, 20
    T_UP, T_DN = [28, 52, 76], [44, 68, 88]
    TL, PL = 96, 48
    MOD_SH1, MOD_G1, MOD_SH2, MOD_SC2, MOD_G2 = 0, 16, 24, 32, 40
    MOD_SC1 = 8

    with ExitStack() as ctx:
        def sb(name, shape, dt=F32):
            return ctx.enter_context(nc.sbuf_tensor(name, shape, dt))

        def sem(name):
            return ctx.enter_context(nc.semaphore(name))

        X = sb("X", [P, KX, 2, HALF])
        NH = sb("norm_hi", [P, KX, 2, HALF], F32R)
        NL = sb("norm_lo", [P, KX, 2, HALF], F32R)
        MH = sb("mid_hi", [P, 8, 2, HALF], F32R)
        ML = sb("mid_lo", [P, 8, 2, HALF], F32R)
        RAW = sb("w_raw", [P, 2, 8, 256])
        WH = sb("w_hi", [P, 2, 8, 256], F32R)
        WL = sb("w_lo", [P, 2, 8, 256], F32R)
        AW = sb("ada_w", [P, 2048])
        CT = sb("silu_c", [P, KX, 32])
        VEC = sb("vec", [P, L, VN])
        CUR = sb("vec_now", [P, VN])
        MOD = sb("mod", [P, 6 * KX, NJ])
        GS = sb("gain", [P, KX, NJ])
        BNEXT = sb("bias_next", [P, 16])
        ADS = sb("ada_rows", [P, 512])
        BLK = sb("gate_w", [P, 2, KH, P])
        IDN = sb("ident", [P, P])
        ONE = sb("ones", [P, P])
        AVG = sb("avg", [P, 1])
        EPST = sb("eps", [P, 1])
        STD = sb("std", [P, 6])
        RST = sb("rstd", [P, 6])
        NS = sb("new_states", [P, NN])
        SMALL = sb("small", [P, 160])
        XTMP = sb("x_tmp", [P, 2, NST_])
        WORK = sb("work", [P, 15 * PADW])

        def wk(i):
            return WORK[:, i * PADW:(i + 1) * PADW]

        CIN = [wk(0), wk(1)]
        XC = [wk(2 + c) for c in range(KH)]
        Z = [wk(6 + c) for c in range(KH)]
        TR, TI, TT = wk(10), wk(11), wk(12)
        HID = [wk(13), wk(14)]
        UC, GE = [wk(2), wk(3)], [wk(4), wk(5)]
        ACC = wk(14)[:, 0:TOK]
        SQ = [wk(11)[:, 0:TOK], wk(12)[:, 0:TOK]]
        SQ0 = [NS[:, 0:TOK], CUR[:, 0:TOK]]
        RSS = wk(4)[:, 0:TOK]
        T1 = [wk(3)[:, 0:TOK], wk(5)[:, 0:TOK]]
        DIAG = WORK[:, 13 * PADW:13 * PADW + 6 * P].rearrange("p (i n) -> p i n", i=6)
        NSR = WORK[:, 7 * PADW:7 * PADW + 6 * P].rearrange("p (i n) -> p i n", i=6)
        FGB = WORK[:, 0:D]
        XROW = WORK[:, 0:6 * D].rearrange("p (a n) -> p a n", a=6)
        VROW = WORK[:, 6 * D:6 * D + 15 * P].rearrange("p (a n) -> p a n", a=15)
        RAWF = [RAW[:, i].rearrange("p k n -> p (k n)") for i in range(2)]
        EARLY = [(AW[:], None), (RAWF[0], None), (RAWF[1], None), (WORK[:, 0:2048], None), (WORK[:, 2048:4096], None),
                 (WORK[:, 4096:6144], None), (AW[:], 0), (WORK[:, 0:2048], 3)]
        YROW = [RAW[:, i // 2].rearrange("p k n -> p (k n)")[:, (i % 2) * D:(i % 2 + 1) * D] for i in range(4)] \
            + [AW[:, 0:D], AW[:, D:2 * D]]

        PS = ctx.enter_context(nc.psum_tensor("ps", [P, 8, 512], F32))
        B_R, B_I, B_MISC, B_ADA = 4, 5, 6, 7

        def halves(t):
            return t[:, 0:TOK].rearrange("p (h n) -> p h n", h=2)

        def pr(t3):
            return t3[:, :, 0:HP]

        def sm(t3):
            return t3[:, :, HP:HALF].rearrange("p h (b t) -> p h b t", t=TS)

        def pp(t):
            return t[:, PADS:SB0].rearrange("p (h n) -> p h n", h=2)

        def spad(t):
            return t[:, SB0:PADW].rearrange("p (b n) -> p b n", b=NB)

        def sp4(t):
            return t[:, SB0:PADW].rearrange("p (h b n) -> p h b n", h=2, b=HB)[:, :, :, PADS:SW]

        def slot(s):
            return PS[:, 2 * s:2 * s + 2, 0:HALF]

        def perseq(v):
            return v.rearrange("p (h b u) -> p h b u", h=2, u=1).broadcast_to([P, 2, HB, TS])

        def token_tiles():
            return [(i, i // 2, (i % 2) * P, P) if i < 4 else (i, i - 4, HP, HS) for i in range(6)]

        tile_done = sem("tile_done")
        psum_free = [sem("psum_free0"), sem("psum_free1")]
        raw_full = [sem("raw_full0"), sem("raw_full1")]
        hi_done, lo_done = sem("hi_done"), sem("lo_done")
        ada_w_full, ada_slices = sem("ada_w_full"), sem("ada_slices")
        ada_rows_ready, ada_cols_done, mod_ready = sem("ada_rows_ready"), sem("ada_cols_done"), sem("mod_ready")
        blk_full, gate_done, gate_read, xc_ready = sem("blk_full"), sem("gate_done"), sem("gate_read"), sem("xc_ready")
        lru_act, m2_ready, scan_ready = sem("lru_act"), sem("m2_ready"), sem("scan_ready")
        conv_out, gelu_out = sem("conv_out"), sem("gelu_out")
        lru_prod, prod_hi, mid_ready = sem("lru_prod"), sem("prod_hi"), sem("mid_ready")
        norm_f, norm_hi, norm_ready = sem("norm_f"), sem("norm_hi_ready"), sem("norm_ready")
        x_ready, sq_ready, acc_ready = sem("x_ready"), sem("sq_ready"), sem("acc_ready")
        stat_done, std_ready, diag_ready, rs_done = sem("stat_done"), sem("std_ready"), sem("diag_ready"), sem("rs_done")
        ns_ready, ns_rows, ns_out, ns_stored = sem("ns_ready"), sem("ns_rows"), sem("ns_out"), sem("ns_stored")
        dve_step, act_step, pool_step = sem("dve_step"), sem("act_step"), sem("pool_step")
        c_in, x_in, ident_ready = sem("c_in"), sem("x_in"), sem("ident_ready")
        c_cols, c_sig, c_ready, v_cols, v_ready = sem("c_cols"), sem("c_sig"), sem("c_ready"), sem("v_cols"), sem("v_ready")
        x_cols, lam_e = sem("x_cols"), sem("lam_e")
        x_copied = sem("x_copied")
        fg_in, y_cols, y_rows, y_out = sem("fg_in"), sem("y_cols"), sem("y_rows"), sem("y_out")
        early_full = [sem(f"early_full{k}") for k in range(KX)]
        v_in = [sem(f"v_in{l}") for l in range(L)]
        t1_ready, rs_copied, ns_read = sem("t1_ready"), sem("rs_copied"), sem("ns_read")
        NVEC = 16

        block = ctx.enter_context(nc.Block())

        def done(l, t):
            return l * TL + t + 5

        def read(l, t):
            return l * (TL // 2) + t // 2 + 2

        def vectors(engine, l):
            def rows(name):
                return a[name][l].rearrange("(k p) -> k p", p=P)
            fs = a["state_ffn_conv"][l].rearrange("b k (c p) -> (b k c) p", p=P)
            for i, r, src in (
                    (0, V_BADA, rows("b_ada")), (0, V_N1, rows("norm1_g")), (0, V_N2, rows("norm2_g")),
                    (0, V_CW, a["lru_conv_w"][l].rearrange("k (c p) -> (k c) p", p=P)),
                    (0, V_CB, rows("lru_conv_b")), (0, V_BA, rows("lru_ba")), (0, V_BX, rows("lru_bx")),
                    (0, V_LAM, rows("lru_lambda")),
                    (0, V_SW, a["sc_conv_w"][l].rearrange("k (c p) -> (k c) p", p=P)),
                    (1, 0, a["ffn_conv_w"][l].rearrange("k (c p) -> (k c) p", p=P)),
                    (1, V_SH - V_FW, a["state_lru_h"][l].rearrange("b (c p) -> (b c) p", p=P)),
                    (2, 0, a["state_lru_conv"][l].rearrange("b k (c p) -> (b k c) p", p=P)),
                    (3, 0, a["state_sc_conv"][l].rearrange("b k (c p) -> (b k c) p", p=P)),
                    (4, 0, fs[0:128]), (5, 0, fs[128:256]), (6, 0, fs[256:352])):
                engine.dma_start(VROW[r:r + src.shape[0], 7 * l + i, :], src).then_inc(v_in[l], 16)

        @block.sync
        def _(sp):
            for r, src in ((0, a["c_prompt"]), (8, a["c_sample"])):
                src = src.rearrange("b (k p) -> (b k) p", p=P)
                sp.dma_start(VROW[r:r + src.shape[0], 14, :], src).then_inc(c_in, 16)
            sp.dma_start(XROW[:, 0:4, :], a["x_prompt"][0].rearrange("(a p) n -> p a n", p=P)).then_inc(x_in, 16)
            xs = a["x_sample"].rearrange("b t n -> (b t) n")
            for h in range(2):
                sp.dma_start(XROW[0:HS, 4 + h, :], xs[h * HS:(h + 1) * HS, :]).then_inc(x_in, 16)

            ada0 = a["w_ada"][0].rearrange("(k p) c -> k p c", p=P)
            for k, (dst, after) in enumerate(EARLY):
                if k == 3:
                    sp.wait_ge(x_cols, KX)
                if after is not None:
                    sp.wait_ge(ada_slices, after + 2)
                sp.dma_start(dst, ada0[k, :, 0:2048]).then_inc(early_full[k], 16)
            sp.wait_ge(ada_slices, 4)

            def load(p, s, src):
                src = src.rearrange("o (k p) c -> p (o k) c", p=P)
                sp.wait_ge(lo_done, p + 1)
                sp.dma_start(RAW[:, s, 0:src.shape[1], :], src).then_inc(raw_full[s], 16)

            load(0, 0, a["w_in"][0:1, :, 0:256])
            with sp.Fori(0, L) as l:
                load(l * PL + 1, 1, a["w_in"][bass.ds(l, 1), :, 256:512])
                n = 2
                for c0 in (3 * DH, 4 * DH, 2 * DH, DH):
                    for s in range(2):
                        load(l * PL + n, s, a["w_in"][bass.ds(l, 1), :, c0 + 256 * s:c0 + 256 * s + 256])
                        n += 1
                for j in range(4):
                    load(l * PL + n, j % 2, a["w_out"][bass.ds(l, 1), :, 256 * j:256 * j + 256])
                    n += 1
                for g, K in enumerate(GROUPS):
                    with sp.Fori(0, K // 2) as q:
                        for s in range(2):
                            load(l * PL + q * 2 + (n + s), s,
                                 a["ffn_w_up"][bass.ds(l, 1), :, bass.ds(q * 256 + (8 * g * P + s * DFF), 256)])
                    n += K
                    for j in range(4):
                        load(l * PL + n, j % 2,
                             a["ffn_w_down"][bass.ds(l, 1), 8 * g * P:(8 * g + K) * P, 256 * j:256 * j + 256])
                        n += 1
                assert n == PL
                after = l * -1 + (L - 1)
                load(l * PL + n, 0, a["w_in"][bass.ds(after, 1), :, 0:256])
            sp.wait_ge(lo_done, L * PL + 3)
            sp.dma_start(FGB, a["final_g"].rearrange("(u n) -> u n", u=1).broadcast_to([P, D])).then_inc(fg_in, 16)
            ys = o["y_sample"].rearrange("b t n -> (b t) n")
            for i, h, t0, w in token_tiles():
                sp.wait_ge(y_rows, i + 1)
                dst = o["y_prompt"][0, i * P:(i + 1) * P, :] if i < 4 else ys[h * HS:(h + 1) * HS, :]
                sp.dma_start(dst, YROW[i][0:w, :]).then_inc(y_out, 16)
            sp.wait_ge(y_out, 16 * 6)

        @block.gpsimd
        def _(pool):
            pool.sem_inc(ns_stored, 1)
            nc.gpsimd.memset(IDN[:], 0.0).then_inc(pool_step, 1)
            pool.wait_ge(pool_step, 1)
            nc.gpsimd.affine_select(out=IDN[:], in_=IDN[:], compare_op=ALU.not_equal, fill=1.0, base=0,
                                    pattern=[[-1, P]], channel_multiplier=1).then_inc(ident_ready, 1)
            nc.gpsimd.memset(ONE[:], 1.0).then_inc(ident_ready, 1)
            nc.gpsimd.memset(AVG[:], 1.0 / D).then_inc(ident_ready, 1)
            nc.gpsimd.memset(EPST[:], EPS).then_inc(ident_ready, 1)
            for l in range(1, L):
                vectors(pool, l)
            nc.gpsimd.memset(BLK[:], 0.0).then_inc(pool_step, 1)

            def ada_load(n, l, r, k):
                chunk = l * KX + k
                pool.wait_ge(ada_slices, n + 1)
                pool.dma_start(AW[:], a["w_ada"].rearrange("l (k p) c -> (l k) p c", p=P)
                               [bass.ds(chunk, 1), :, r * 2048:(r + 1) * 2048]
                               .rearrange("o p c -> p (o c)")).then_inc(ada_w_full, 16)

            pool.wait_ge(pool_step, 2)
            with pool.Fori(0, L) as l:
                pool.wait_ge(gate_done, l * 8 + 1)
                for m, w in enumerate(("lru_wa", "lru_wx")):
                    for q in range(2):
                        src = a[w][bass.ds(l, 1)].rearrange("o (c q) i j -> q i (o c) j", q=2)[q]
                        pool.dma_start(BLK[q * HD:(q + 1) * HD, m, :, q * HD:(q + 1) * HD], src).then_inc(blk_full, 16)
                after = l * -1 + (L - 1)
                for i, (lr, r) in enumerate(((l, 1), (l, 2), (after, 0))):
                    with pool.Fori(0, KX) as k:
                        ada_load(l * 24 + k + (8 + 8 * i), lr, r, k)
                pool.wait_ge(ns_read, l * 6 + 6)
                for name, i, r, n, r0 in NSO:
                    dst = o["new_" + name][bass.ds(l, 1)]
                    dst = dst.rearrange("o b (c p) -> (o b c) p", p=P) if len(dst.shape) == 3 else \
                        dst.rearrange("o b k (c p) -> (o b k c) p", p=P)
                    pool.dma_start(dst[r0:r0 + n], NSR[r:r + n, i, :]).then_inc(ns_out, 16)
                pool.wait_ge(ns_out, l * (16 * len(NSO)) + 16 * len(NSO))
                pool.sem_inc(ns_stored, 1)

        @block.tensor
        def _(pe):
            T = nc.tensor
            pe.sem_inc(tile_done, 4)
            pe.sem_inc(ada_slices, 1)
            pe.sem_inc(gate_done, 1)

            def chunk(i, s, k, xh, xl, start, stop):
                r, c = i // 2, (i % 2) * P
                for h in range(2):
                    out = PS[:, 2 * s + h, 0:HALF]
                    T.matmul(out, WH[:, r, k, c:c + P], xh[:, k, h, :], start=start, stop=False)
                    T.matmul(out, WH[:, r, k, c:c + P], xl[:, k, h, :], start=False, stop=False)
                    last = T.matmul(out, WL[:, r, k, c:c + P], xh[:, k, h, :], start=False, stop=stop)
                return last

            def tile(pair, i, xh, xl, order, ready=None):
                if i % 2 == 0:
                    pe.wait_ge(lo_done, pair + (i // 2 + 3))
                pe.wait_ge(psum_free[i % 2], pair + (i // 2 + 1))
                for j, k in enumerate(order):
                    if ready is not None:
                        pe.wait_ge(ready[0], ready[1] + (j + 1))
                    last = chunk(i, i % 2, k, xh, xl, j == 0, j == len(order) - 1)
                last.then_inc(tile_done, 1)

            def first_quad(pair, ready, rs):
                half = KX // 2
                for k, tiles in [(k, range(4)) for k in range(half)] + \
                        [(k, t) for t in ((0, 1), (2, 3)) for k in range(half, KX)]:
                    if 0 in tiles:
                        pe.wait_ge(norm_ready, ready + (k + 1))
                    for i in tiles:
                        if k == 0:
                            if i % 2 == 0:
                                pe.wait_ge(lo_done, pair + (i // 2 + 3))
                            if i < 2:
                                pe.wait_ge(psum_free[i], pair + 1)
                            if i == 3:
                                pe.wait_ge(rs_copied, rs)
                        last = chunk(i, i, k, NH, NL, k == 0, k == KX - 1)
                        if k == KX - 1:
                            last.then_inc(tile_done, 1)

            def ada_slice(n, k):
                src = EARLY[k][0] if n is None else AW
                if n is None:
                    pe.wait_ge(early_full[k], 16)
                else:
                    pe.wait_ge(ada_w_full, (n - KX) * 16 + 16)
                for g in range(4):
                    last = T.matmul(PS[32 * g:32 * g + 32, B_ADA, :], CT[:, k, :], src[:, g * 512:(g + 1) * 512],
                                    start=(k == 0), stop=(k == KX - 1))
                last.then_inc(ada_slices, 1)

            def ada_turn(m):
                pe.wait_ge(ada_rows_ready, m)
                for q in range(4):
                    last = T.transpose(PS[:, B_MISC, q * P:(q + 1) * P], ADS[:, q * P:(q + 1) * P], IDN[:])
                last.then_inc(ada_cols_done, 1)

            def norm_stats(m):
                pe.wait_ge(acc_ready, m)
                for i, h, t0, w in token_tiles():
                    last = T.matmul(PS[0:w, B_ADA, i:i + 1], ACC[:, h * HALF + t0:h * HALF + t0 + w], AVG[:],
                                    start=True, stop=True)
                last.then_inc(stat_done, 1)

            def norm_spread(m):
                pe.wait_ge(diag_ready, m)
                for i, h, t0, w in token_tiles():
                    last = T.matmul(PS[:, 6 + h, t0:t0 + w], ONE[0:w, :], DIAG[0:w, i, 0:w], start=True, stop=True)
                last.then_inc(rs_done, 1)

            pe.wait_ge(ident_ready, 4)
            pe.wait_ge(c_in, 32)
            T.transpose(PS[:, B_MISC, 0:72], VROW[0:72, 14, :], IDN[0:72, 0:72]).then_inc(c_cols, 1)
            pe.wait_ge(x_in, 48)
            for k in range(KX):
                if k >= 2:
                    pe.wait_ge(x_copied if k % 2 else x_ready, k // 2)
                for i, h, t0, w in token_tiles():
                    last = T.transpose(PS[:, 2 * (k % 2) + h, t0:t0 + w], XROW[0:w, i, k * P:(k + 1) * P], IDN[0:w, 0:w])
                last.then_inc(x_cols, 1)
            for l in range(L):
                pe.wait_ge(v_in[l], 16 * NVEC)
                if l:
                    pe.wait_ge(x_ready, KX // 2)
                for i, n, b, c in VT:
                    last = T.transpose(PS[:, b - 4 * l, c:c + n], VROW[0:n, 7 * l + i, :], IDN[0:n, 0:n])
                last.then_inc(v_cols, 1)
            norm_stats(1)
            pe.wait_ge(c_ready, 1)
            pe.wait_ge(std_ready, 1)
            for k in range(KX):
                ada_slice(None, k)
            ada_turn(1)

            with pe.Fori(0, L) as l:
                pe.wait_ge(mod_ready, l * 3 + 1)
                norm_spread(l * 2 + 1)
                first_quad(l * PL, l * 16, l * 2 + 1)
                for t in range(4, T_UP[0]):
                    if t < T_WOUT:
                        tile(l * PL + t // 4 * 2, t % 4, NH, NL, range(KX))
                    else:
                        tile(l * PL + t // 4 * 2, t % 4, MH, ML, [4, 5, 6, 7, 0, 1, 2, 3],
                             (mid_ready, l * 30) if t == T_WOUT else None)
                    if t in (12, 20):
                        if t == 12:
                            pe.wait_ge(gate_read, l * 8 + 4)
                        ada_turn(l * 3 + (2 if t == 12 else 3))
                    i, k = (t - 4) // 8, (t - 4) % 8
                    if t == 4:
                        pe.wait_ge(psum_free[1], l * PL + 3)
                    if k == 0:
                        pe.wait_ge(ada_rows_ready, l * 3 + (i + 1))
                    ada_slice(l * 24 + (8 + 8 * i + k), k)
                    if t in (9, 11, 13, 15):
                        c = (t - 9) // 2
                        pe.wait_ge(xc_ready, l * 4 + (c + 1))
                        if c == 0:
                            pe.wait_ge(blk_full, l * 64 + 64)
                        else:
                            if c == 2:
                                pe.wait_ge(mod_ready, l * 3 + 2)
                            pe.wait_ge(gate_read, l * 8 + 2 * c)
                        for m, b in ((0, B_R), (1, B_I)):
                            T.matmul(PS[:, b, :], BLK[:, m, c, :], XC[c][:, PADS:SB0], start=True, stop=True)
                            T.matmul(PS[:, B_MISC, m * NST_:(m + 1) * NST_], BLK[:, m, c, :],
                                     spad(XC[c])[:, :, PADS:SW], start=True, stop=True).then_inc(gate_done, 1)
                pe.wait_ge(ada_rows_ready, l * 3 + 4)
                norm_stats(l * 2 + 2)
                pe.wait_ge(mod_ready, l * 3 + 3)
                norm_spread(l * 2 + 2)
                first_quad(l * PL + T_UP[0] // 2, l * 16 + 8, l * 2 + 2)
                made = 8
                for g, K in enumerate(GROUPS):
                    with pe.Fori(1 if g == 0 else 0, K // 2) as q:
                        for i in range(4):
                            tile(l * PL + q * 2 + T_UP[g] // 2, i, NH, NL, range(KX))
                    if g == 0:
                        ada_turn(l * 3 + 4)
                    with pe.Fori(0, 2 if g < 2 else 1) as q:
                        for i in range(4):
                            tile(l * PL + q * 2 + T_DN[g] // 2, i, MH, ML, range(K),
                                 (mid_ready, l * 30 + made) if i == 0 else None)
                    if g == 2:
                        pe.wait_ge(ns_ready, l + 1)
                        pe.wait_ge(mod_ready, l * 3 + 4)
                        for i, (c0, n) in enumerate(NST):
                            last = T.transpose(PS[0:n, B_MISC if i < 4 else B_R, (i % 4) * P:(i % 4 + 1) * P],
                                               NS[:, c0:c0 + n], IDN[:])
                        last.then_inc(ns_rows, 1)
                        for i in range(4):
                            tile(l * PL + T_DN[g] // 2 + 2, i, MH, ML, range(K))
                    made += K
                pe.wait_ge(ns_read, l * 6 + 6)
                norm_stats(l * 2 + 3)
            for i, h, t0, w in token_tiles():
                s = i % 3
                if i >= 3:
                    pe.wait_ge(y_rows, i - 2)
                for k in range(KX):
                    last = T.transpose(PS[0:w, 2 * s + k // 4, (k % 4) * P:(k % 4 + 1) * P], X[:, k, h, t0:t0 + w], IDN[:])
                last.then_inc(y_cols, 1)

        @block.scalar
        def _(act):
            A = nc.scalar.activation
            vectors(act, 0)

            def split(l, n, q=0):
                s = n % 2
                act.wait_ge(raw_full[s], l * (8 * PL) + q * 16 + 16 * (n // 2 + 1))
                act.wait_ge(tile_done, l * TL + q * 4 + (2 * n + 2))
                A(WH[:, s], RAW[:, s], ACT.Copy).then_inc(hi_done, 1)

            def ada_rows(m, first=False):
                act.wait_ge(ada_slices, m * 8 + 1)
                if not first:
                    act.wait_ge(ada_cols_done, m - 1)
                A(ADS[:], PS[:, B_ADA, :], ACT.Copy).then_inc(ada_rows_ready, 1)

            def std(m):
                act.wait_ge(stat_done, m)
                A(STD[:, 0:4], PS[:, B_ADA, 0:4], ACT.Sqrt, bias=EPST[:])
                A(STD[0:HS, 4:6], PS[0:HS, B_ADA, 4:6], ACT.Sqrt, bias=EPST[0:HS, :]).then_inc(std_ready, 1)

            def square(n, m):
                act.wait_ge(x_ready, n + (m + 1))
                A(halves(SQ[m % 2]), X[:, m], ACT.Square).then_inc(sq_ready, 1)

            def norm_round(m, n, sh):
                for k in range(KX):
                    act.wait_ge(t1_ready, n + (k + 1))
                    if k == 1:
                        A(halves(RSS), PS[:, 6:8, 0:HALF], ACT.Copy).then_inc(rs_copied, 1)
                    A(pr(NH[:, k]), pr(halves(T1[k % 2])), ACT.Identity, scale=GS[:, k, 0:1], bias=MOD[:, sh + k, 0:1])
                    act.wait_ge(norm_f, n + (k + 1))
                    A(NH[:, k, :, HP:HALF], halves(HID[k % 2])[:, :, HP:HALF], ACT.Copy).then_inc(norm_hi, 1)

            act.wait_ge(c_cols, 1)
            A(SMALL[:, 0:72], PS[:, B_MISC, 0:72], ACT.Sigmoid).then_inc(c_sig, 1)
            act.preload_act_table(ACT.Sqrt)
            for k in range(KX):
                if k % 2:
                    act.wait_ge(x_cols, k + 1)
                    A(X[:, k], slot(1), ACT.Copy).then_inc(x_copied, 1)
                    act.wait_ge(x_copied, k // 2 + 1)
                else:
                    act.wait_ge(x_ready, k // 2 + 1)
                if k >= 2:
                    act.wait_ge(dve_step, k + 2)
                A(halves(SQ0[k % 2]), X[:, k], ACT.Square).then_inc(sq_ready, 1)
            std(1)
            for l in range(L):
                act.wait_ge(v_cols, l + 1)
                A(VEC[:, l, 0:366], PS[:, 4 - 4 * l, 0:366], ACT.Copy).then_inc(v_ready, 1)
                A(VEC[:, l, 366:718], PS[:, 5 - 4 * l, 0:352], ACT.Copy).then_inc(v_ready, 1)
            act.wait_ge(v_ready, 2 * L)
            for l in range(L):
                A(SMALL[:, 80 + 4 * l:84 + 4 * l], VEC[:, l, V_LAM:V_LAM + 4], ACT.Abs).then_inc(act_step, 1)
            act.wait_ge(act_step, L)
            A(SMALL[:, 88:96], SMALL[:, 80:88], ACT.Exp, scale=-1.0).then_inc(lam_e, 1)
            act.preload_act_table(ACT.Sqrt)
            ada_rows(1, first=True)
            split(0, 0)

            with act.Fori(0, L) as l:
                split(l, 1)
                norm_round(l * 2 + 1, l * 16, MOD_SH1)
                for c in range(KH):
                    act.wait_ge(tile_done, done(l, c))
                    if c >= 2:
                        act.wait_ge(xc_ready, l * 4 + (c - 1))
                    A(pp(CIN[c % 2]), pr(slot(c)), ACT.Copy)
                    A(sp4(CIN[c % 2]), sm(slot(c)), ACT.Copy).then_inc(psum_free[c % 2], 1)
                    if c == 1:
                        split(l, 2)
                split(l, 3)
                act.wait_ge(ns_stored, l + 1)
                for c in range(KH):
                    act.wait_ge(tile_done, done(l, T_CS + c))
                    A(pp(Z[c]), pr(slot(c % 2)), ACT.Copy)
                    A(sp4(Z[c]), sm(slot(c % 2)), ACT.Copy).then_inc(psum_free[c % 2], 1)
                    if c == 1:
                        split(l, 4)
                split(l, 5)

                def gates(c):
                    if c:
                        act.wait_ge(scan_ready, l * 4 + c)
                    act.wait_ge(gate_done, l * 8 + (2 * c + 3))
                    for m, (row, b, v) in enumerate(((TR, B_R, V_BA), (TI, B_I, V_BX))):
                        bias = CUR[:, v + c:v + c + 1]
                        A(row[:, PADS:SB0], PS[:, b, :], ACT.Sigmoid, bias=bias)
                        A(spad(row)[:, :, PADS:SW], PS[:, B_MISC, m * NST_:(m + 1) * NST_].rearrange("p (b t) -> p b t", t=TS),
                          ACT.Sigmoid, bias=bias).then_inc(gate_read, 1)
                    act.wait_ge(gate_read, l * 8 + (2 * c + 2))
                    A(TT[:, PADS:], TR[:, PADS:], ACT.Tanh, scale=CUR[:, V_SP + c:V_SP + c + 1])
                    A(TR[:, PADS:], TR[:, PADS:], ACT.Exp, scale=CUR[:, V_NSP + c:V_NSP + c + 1]).then_inc(lru_act, 1)

                def root(c):
                    act.wait_ge(m2_ready, l * 4 + (c + 1))
                    A(TT[:, PADS:], TT[:, PADS:], ACT.Sqrt).then_inc(lru_act, 1)

                def sc_round(c):
                    act.wait_ge(psum_free[c % 2], read(l, T_BS + c))
                    A(MH[:, 4 + c], halves(HID[c % 2]), ACT.Copy).then_inc(prod_hi, 1)

                gates(0)
                root(0)
                split(l, 6)
                ada_rows(l * 3 + 2)
                gates(1)
                root(1)
                split(l, 7)
                sc_round(0)
                split(l, 8)
                gates(2)
                sc_round(1)
                root(2)
                sc_round(2)
                split(l, 9)
                gates(3)
                sc_round(3)
                root(3)
                for c in range(KH):
                    act.wait_ge(tile_done, done(l, T_GL + c))
                    if c >= 2:
                        act.wait_ge(lru_prod, l * 4 + (c - 1))
                    A(CIN[c % 2][:, PADS:PADS + TOK].rearrange("p (h n) -> p h n", h=2), slot(c % 2),
                      ACT.Gelu_apprx_tanh).then_inc(psum_free[c % 2], 1)
                    if c == 1:
                        split(l, 10)
                    act.wait_ge(lru_prod, l * 4 + (c + 1))
                    A(MH[:, c], halves(HID[c % 2]), ACT.Copy).then_inc(prod_hi, 1)
                ada_rows(l * 3 + 3)
                split(l, 11)
                act.preload_act_table(ACT.Sqrt)
                for m in range(KX):
                    if m == 7:
                        ada_rows(l * 3 + 4)
                    square(l * 16 + 4, m)
                    if m in (1, 3, 5):
                        split(l, 12 + m // 2)
                std(l * 2 + 2)
                split(l, T_UP[0] // 2 + 1)
                act.preload_act_table(ACT.Gelu_apprx_tanh)
                norm_round(l * 2 + 2, l * 16 + 8, MOD_SH2)

                def up_quad(g, q, made, v_slot):
                    if v_slot == 0:
                        split(l, T_UP[g] // 2 + 1, q)
                    for e in range(2):
                        act.wait_ge(tile_done, l * TL + q * 4 + (T_UP[g] + e + 5))
                        A(pp(CIN[e]), pr(slot(e)), ACT.Copy)
                        A(sp4(CIN[e]), sm(slot(e)), ACT.Copy).then_inc(psum_free[e], 1)
                    split(l, T_UP[g] // 2 + 2, q)
                    for e in range(2):
                        act.wait_ge(conv_out, l * KF + q * 2 + (made + e + 1))
                        A(GE[e][:, PADS:], UC[e][:, PADS:], ACT.Gelu_apprx_tanh).then_inc(gelu_out, 1)
                    for e in range(2):
                        act.wait_ge(psum_free[e], l * PL + q * 2 + (T_UP[g] // 2 + 3))
                        A(MH[:, bass.ds(q * 2 + e, 1)].rearrange("p o h n -> p (o h) n"), halves(HID[e]), ACT.Copy)\
                            .then_inc(prod_hi, 1)

                made = 0
                for g, K in enumerate(GROUPS):
                    if g:
                        act.preload_act_table(ACT.Gelu_apprx_tanh)
                    else:
                        up_quad(0, 0, 0, 2)
                    with act.Fori(1 if g == 0 else 0, K // 2) as q:
                        up_quad(g, q, made, 0)
                    nd = T_DN[g] // 2
                    split(l, nd + 1)
                    if g < 2:
                        for n in range(nd + 2, nd + 5):
                            split(l, n)
                    else:
                        act.preload_act_table(ACT.Sqrt)
                        for m in range(KX):
                            square(l * 16 + 12, m)
                            if m in (1, 3):
                                split(l, nd + 2 + m // 2)
                            if m == 5:
                                split(l, PL)
                            if m == 4:
                                act.wait_ge(ns_rows, l + 1)
                                for i, (c0, n) in enumerate(NST):
                                    A(NSR[0:n, i, :], PS[0:n, B_MISC if i < 4 else B_R, (i % 4) * P:(i % 4 + 1) * P],
                                      ACT.Copy).then_inc(ns_read, 1)
                        std(l * 2 + 3)
                    made += K

        @block.vector
        def _(dve):
            V = nc.vector

            class Steps:
                base, n = 0, 0

                def __call__(self, ins):
                    ins.then_inc(dve_step, 1)
                    self.n += 1
                    dve.wait_ge(dve_step, self.base + self.n)

            step = Steps()
            dve.sem_inc(lo_done, 2)
            dve.sem_inc(psum_free[0], 1)
            dve.sem_inc(psum_free[1], 1)

            def split(l, n, q=0):
                s = n % 2
                dve.wait_ge(hi_done, l * PL + q * 2 + (n + 1))
                V.tensor_tensor(WL[:, s], RAW[:, s], WH[:, s].bitcast(F32), ALU.subtract).then_inc(lo_done, 1)

            def low(dst_lo, src, hi, signal):
                V.tensor_tensor(dst_lo, src, hi.bitcast(F32), ALU.subtract).then_inc(signal, 1)

            def product(row, g2, g4, src, signal):
                V.tensor_tensor(pr(halves(row)), g2, pr(src), ALU.mult)
                V.tensor_tensor(sm(halves(row)), g4, sm(src), ALU.mult).then_inc(signal, 1)

            def modulation(m, c0, bias):
                dve.wait_ge(ada_cols_done, m)
                out = MOD[:, c0:c0 + 16, :].rearrange("p (g q) j -> p g q j", g=4)
                src = PS[:, B_MISC, :].rearrange("p (q g j) -> p g q j", q=4, g=4)[:, :, :, 0:NJ]
                b = bias.rearrange("p (g q u) -> p g q u", g=4, u=1).broadcast_to([P, 4, 4, NJ])
                V.tensor_tensor(out, src, b, ALU.add).then_inc(mod_ready, 1)

            def gains(c0, v):
                step(V.tensor_scalar(GS[:], MOD[:, c0:c0 + KX, :], 1.0, None, ALU.add))
                g = CUR[:, v:v + KX].rearrange("p (k u) -> p k u", u=1).broadcast_to([P, KX, NJ])
                step(V.tensor_tensor(GS[:], GS[:], g, ALU.mult))

            def sum_square(n, m, sq=SQ):
                dve.wait_ge(sq_ready, n + (m + 1))
                if m == 0:
                    ins = V.tensor_copy(ACC, sq[0])
                else:
                    ins = V.tensor_tensor(ACC, ACC, sq[m % 2], ALU.add)
                if m < KX - 1:
                    step(ins)
                else:
                    ins.then_inc(acc_ready, 1)

            def rstd(m):
                dve.wait_ge(std_ready, m)
                step(V.reciprocal(RST[:], STD[:]))

            def diag(m):
                V.tensor_tensor(DIAG, IDN[:].rearrange("p (u n) -> p u n", u=1).broadcast_to([P, 6, P]),
                                RST[:].rearrange("p (i u) -> p i u", u=1).broadcast_to([P, 6, P]),
                                ALU.mult).then_inc(diag_ready, 1)

            def normalise(m, n, sh):
                def scaled(k):
                    rs = PS[:, 6:8, 0:HALF] if k < 2 else halves(RSS)
                    V.tensor_tensor(halves(T1[k % 2]), X[:, k], rs, ALU.mult).then_inc(t1_ready, 1)
                    dve.wait_ge(t1_ready, n + (k + 1))
                dve.wait_ge(rs_done, m)
                scaled(0)
                for k in range(KX):
                    f, t = halves(HID[k % 2]), halves(T1[k % 2])
                    V.tensor_tensor(sm(f), sm(t), perseq(GS[:, k, 1:NJ]), ALU.mult)
                    step(V.tensor_scalar(pr(f), pr(t), GS[:, k, 0:1], MOD[:, sh + k, 0:1], ALU.mult, ALU.add))
                    V.tensor_tensor(sm(f), sm(f), perseq(MOD[:, sh + k, 1:NJ]), ALU.add).then_inc(norm_f, 1)
                    if k < KX - 1:
                        if k == 1:
                            dve.wait_ge(rs_copied, m)
                        scaled(k + 1)
                    dve.wait_ge(norm_hi, n + (k + 1))
                    low(NL[:, k], halves(HID[k % 2]), NH[:, k], norm_ready)

            def residual(wait, s, xm, mod, free, signal=None):
                dve.wait_ge(tile_done, wait)
                V.scalar_tensor_tensor(out=pr(xm), in0=pr(slot(s)), scalar=mod(0, 1), in1=pr(xm),
                                       op0=ALU.mult, op1=ALU.add)
                tmp = XTMP[:, s].rearrange("p (h b t) -> p h b t", h=2, t=TS)
                V.tensor_tensor(tmp, sm(slot(s)), perseq(mod(1, NJ)), ALU.mult).then_inc(psum_free[s], 1)
                dve.wait_ge(psum_free[s], free)
                ins = V.tensor_tensor(sm(xm), sm(xm), tmp, ALU.add)
                if signal is None:
                    step(ins)
                else:
                    ins.then_inc(signal, 1)

            def conv3(out, row, w):
                step(V.tensor_scalar(out[:, PADS:], row[:, PADS:], w(2), None, ALU.mult))
                for k in range(2):
                    ins = V.scalar_tensor_tensor(out=out[:, PADS:], in0=row[:, k + 1:PADW - 2 + k], scalar=w(k),
                                                 in1=out[:, PADS:], op0=ALU.mult, op1=ALU.add)
                    if k == 0:
                        step(ins)
                return ins

            step(V.memset(CT[:], 0.0))
            step(V.memset(STD[:], 1.0))
            dve.wait_ge(c_sig, 1)
            step(V.tensor_tensor(CT[:, :, 0], PS[:, B_MISC, 0:8], SMALL[:, 0:8], ALU.mult))
            (V.tensor_tensor(CT[:, :, 1:NJ], PS[:, B_MISC, 8:72].rearrange("p (b k) -> p k b", k=KX),
                                 SMALL[:, 8:72].rearrange("p (b k) -> p k b", k=KX), ALU.mult)).then_inc(c_ready, 1)
            for k in range(KX):
                if k % 2 == 0:
                    dve.wait_ge(x_cols, k + 1)
                    V.tensor_copy(X[:, k], slot(0)).then_inc(x_ready, 1)
                if k:
                    sum_square(0, k - 1, SQ0)
            sum_square(0, KX - 1, SQ0)
            dve.wait_ge(lam_e, 1)
            E, Zs, Z2, Q, M0 = (SMALL[:, c:c + 8] for c in (88, 96, 104, 112, 120))
            step(V.tensor_scalar(Q, E, 2.0, None, ALU.add))
            step(V.reciprocal(Q, Q))
            step(V.tensor_tensor(Zs, E, Q, ALU.mult))
            step(V.tensor_tensor(Z2, Zs, Zs, ALU.mult))
            step(V.tensor_scalar(Q, Z2, 1.0 / 17, None, ALU.mult))
            for d in (15, 13, 11, 9, 7, 5, 3):
                step(V.scalar_tensor_tensor(out=Q, in0=Q, scalar=1.0 / d, in1=Z2, op0=ALU.add, op1=ALU.mult))
            step(V.scalar_tensor_tensor(out=Q, in0=Q, scalar=1.0, in1=Zs, op0=ALU.add, op1=ALU.mult))
            for l in range(L):
                m0, q0 = M0[:, 4 * l:4 * l + 4], Q[:, 4 * l:4 * l + 4]
                step(V.tensor_scalar(m0, VEC[:, l, V_LAM:V_LAM + 4], -1.0, 0.0, ALU.mult, ALU.max))
                step(V.scalar_tensor_tensor(out=m0, in0=q0, scalar=2.0, in1=m0, op0=ALU.mult, op1=ALU.add))
                step(V.tensor_scalar(VEC[:, l, V_SP:V_SP + 4], m0, RG_C, None, ALU.mult))
                step(V.tensor_scalar(VEC[:, l, V_NSP:V_NSP + 4], m0, -RG_C, None, ALU.mult))
            rstd(1)
            modulation(1, MOD_SH1, VEC[:, 0, 0:16])
            step(V.tensor_copy(CUR[:], VEC[:, 0, :]))
            dve.wait_ge(mod_ready, 1)
            gains(MOD_SC1, V_N1)
            dve.wait_ge(ada_slices, KX + 1)
            for row in Z:
                V.memset(spad(row)[:, :, 0:PADS], 0.0)
            for row in (TR, TI):
                V.memset(row[:, 0:PADS], 0.0)
                V.memset(spad(row)[:, :, 0:PADS], 0.0)
            V.memset(CIN[0][:, 0:PADS], 0.0)
            step(V.memset(CIN[1][:, 0:PADS], 0.0))
            split(0, 0)
            before = step.n

            with dve.Fori(0, L) as l:
                step.base, step.n = l * DVE_STEPS + before, 0
                after = l * -1 + (L - 1)
                diag(l * 2 + 1)
                split(l, 1)
                normalise(l * 2 + 1, l * 16, MOD_SH1)
                slc = CUR[:, V_SLC:V_SLC + 96].rearrange("p (b k c) -> p b k c", k=3, c=KH)
                nlcs = NS[:, N_LCS:N_LCS + 96].rearrange("p (b k c) -> p b k c", k=3, c=KH)
                nlcp = NS[:, N_LCP:N_LCP + 12].rearrange("p (k c) -> p k c", c=KH)
                for c in range(KH):
                    row, s = CIN[c % 2], c % 2
                    step(V.tensor_copy(spad(row)[:, :, 0:3], slc[:, :, :, c]))
                    dve.wait_ge(psum_free[s], read(l, c))
                    V.tensor_copy(nlcp[:, :, c], row[:, SB0 - 3:SB0])
                    V.tensor_copy(nlcs[:, :, :, c], spad(row)[:, :, SW - 3:SW])
                    cw = [CUR[:, V_CW + 4 * k + c:V_CW + 4 * k + c + 1] for k in range(4)]
                    out = XC[c][:, PADS:]
                    step(V.tensor_scalar(out, row[:, PADS:], cw[3], CUR[:, V_CB + c:V_CB + c + 1], ALU.mult, ALU.add))
                    for k in range(3):
                        ins = V.scalar_tensor_tensor(out=out, in0=row[:, k:PADW - 3 + k], scalar=cw[k], in1=out,
                                                     op0=ALU.mult, op1=ALU.add)
                        if k < 2:
                            step(ins)
                    ins.then_inc(xc_ready, 1)
                    if c == 1:
                        split(l, 2)
                split(l, 3)
                dve.wait_ge(ns_stored, l + 1)
                ssc = CUR[:, V_SSC:V_SSC + 64].rearrange("p (b k c) -> p b k c", k=2, c=KH)
                for c in range(KH):
                    step(V.memset(Z[c][:, 0:PADS], 0.0))
                    step(V.tensor_copy(spad(Z[c])[:, :, 1:3], ssc[:, :, :, c]))
                split(l, 4)
                split(l, 5)

                def c_times_h(c):
                    s = c % 2
                    dve.wait_ge(psum_free[s], read(l, T_CS + c))
                    dve.wait_ge(tile_done, done(l, T_HS + c))
                    V.tensor_tensor(pp(Z[c]), pp(Z[c]), pr(slot(s)), ALU.mult)
                    V.tensor_tensor(sp4(Z[c]), sp4(Z[c]), sm(slot(s)), ALU.mult).then_inc(psum_free[s], 1)
                    dve.wait_ge(psum_free[s], read(l, T_HS + c))
                    V.tensor_copy(NS[:, N_SCP:N_SCP + 8].rearrange("p (k c) -> p k c", c=KH)[:, :, c], Z[c][:, SB0 - 2:SB0])
                    V.tensor_copy(NS[:, N_SCS:N_SCS + 64].rearrange("p (b k c) -> p b k c", k=2, c=KH)[:, :, :, c],
                                  spad(Z[c])[:, :, SW - 2:SW])

                def lru_m2(c):
                    dve.wait_ge(lru_act, l * 8 + (2 * c + 1))
                    step(V.tensor_tensor(CIN[1][:, PADS:], TR[:, PADS:], TR[:, PADS:], ALU.mult))
                    V.scalar_tensor_tensor(out=TT[:, PADS:], in0=CIN[1][:, PADS:], scalar=1.0, in1=TT[:, PADS:],
                                           op0=ALU.add, op1=ALU.mult).then_inc(m2_ready, 1)
                    step(V.tensor_tensor(TI[:, PADS:], TI[:, PADS:], XC[c][:, PADS:], ALU.mult))

                def lru_scan(c):
                    dve.wait_ge(lru_act, l * 8 + (2 * c + 2))
                    step(V.tensor_tensor(TI[:, PADS:], TI[:, PADS:], TT[:, PADS:], ALU.mult))
                    step(V.memset(spad(TI)[:, :, 0:2], 0.0))
                    h0 = CUR[:, V_SH:V_SH + 32].rearrange("p (b c) -> p b c", c=KH)
                    step(V.tensor_copy(spad(TI)[:, :, 2], h0[:, :, c]))
                    step(V.memset(spad(TR)[:, :, 0:PADS], 0.0))
                    V.tensor_tensor_scan(XC[c][:, PADS:], TR[:, PADS:], TI[:, PADS:], 0.0, ALU.mult, ALU.add)\
                        .then_inc(scan_ready, 1)
                    dve.wait_ge(scan_ready, l * 4 + (c + 1))
                    V.tensor_copy(NS[:, N_HP + c:N_HP + c + 1], XC[c][:, SB0 - 1:SB0])
                    V.tensor_copy(NS[:, N_HS:N_HS + 32].rearrange("p (b c) -> p b c", c=KH)[:, :, c],
                                  spad(XC[c])[:, :, SW - 1])

                def sc_product(c):
                    s = c % 2
                    step(conv3(CIN[0], Z[c], lambda k: CUR[:, V_SW + 4 * k + c:V_SW + 4 * k + c + 1]))
                    dve.wait_ge(tile_done, done(l, T_BS + c))
                    product(HID[s], pp(CIN[0]), sp4(CIN[0]), slot(s), psum_free[s])

                def sc_low(c):
                    dve.wait_ge(prod_hi, l * 30 + (c + 1))
                    low(ML[:, 4 + c], halves(HID[c % 2]), MH[:, 4 + c], mid_ready)

                c_times_h(0)
                c_times_h(1)
                lru_m2(0)
                c_times_h(2)
                lru_scan(0)
                split(l, 6)
                c_times_h(3)
                lru_m2(1)
                lru_scan(1)
                modulation(l * 3 + 2, 16, CUR[:, 16:32])
                split(l, 7)
                sc_product(0)
                sc_low(0)
                sc_product(1)
                split(l, 8)
                lru_m2(2)
                sc_low(1)
                sc_product(2)
                lru_scan(2)
                sc_low(2)
                sc_product(3)
                split(l, 9)
                lru_m2(3)
                sc_low(3)
                lru_scan(3)
                for c in range(KH):
                    s = c % 2
                    dve.wait_ge(psum_free[s], read(l, T_GL + c))
                    gl = CIN[s][:, PADS:PADS + TOK].rearrange("p (h n) -> p h n", h=2)
                    product(HID[s], pp(XC[c]), sp4(XC[c]), gl, lru_prod)
                    if c == 1:
                        split(l, 10)
                    dve.wait_ge(prod_hi, l * 30 + (c + 5))
                    low(ML[:, c], halves(HID[s]), MH[:, c], mid_ready)
                split(l, 11)
                for m in range(KX):
                    residual(done(l, T_WOUT + m), m % 2, X[:, m], lambda a_, b_, m=m: MOD[:, MOD_G1 + m, a_:b_],
                             read(l, T_WOUT + m), x_ready)
                    if m == 0:
                        modulation(l * 3 + 3, 32, CUR[:, 32:48])
                        dve.wait_ge(mod_ready, l * 3 + 3)
                        gains(MOD_SC2, V_N2)
                    else:
                        sum_square(l * 16 + 8, m - 1)
                    if m in (1, 3, 5):
                        split(l, 12 + m // 2)
                sum_square(l * 16 + 8, KX - 1)
                step(V.tensor_copy(BNEXT[:], VEC[:, bass.ds(after, 1), 0:16].rearrange("p o n -> p (o n)")))
                rstd(l * 2 + 2)
                diag(l * 2 + 2)
                split(l, T_UP[0] // 2 + 1)
                normalise(l * 2 + 2, l * 16 + 8, MOD_SH2)

                ssf = CUR[:, V_SF:V_SF + 352].rearrange("p (b k m) -> p b k m", k=2, m=KF)
                nfs = NS[:, N_FS:N_FS + 352].rearrange("p (b k m) -> p b k m", k=2, m=KF)
                nfp = NS[:, N_FP:N_FP + 44].rearrange("p (k m) -> p k m", m=KF)
                def up_quad(g, q, made, v_slot):
                    if v_slot == 0:
                        split(l, T_UP[g] // 2 + 1, q)
                    for e in range(2):
                        row = CIN[e]
                        ch = bass.ds(q * 2 + (made + e), 1)
                        step(V.tensor_copy(spad(row)[:, :, 1:3], ssf[:, :, :, ch].rearrange("p b k o -> p b (k o)")))
                        dve.wait_ge(psum_free[e], l * PL + q * 2 + (T_UP[g] // 2 + 2))
                        V.tensor_copy(nfp[:, :, ch].rearrange("p k o -> p (k o)"), row[:, SB0 - 2:SB0])
                        V.tensor_copy(nfs[:, :, :, ch].rearrange("p b k o -> p b (k o)"), spad(row)[:, :, SW - 2:SW])
                        conv3(UC[e], row, lambda k: CUR[:, bass.ds(q * 2 + (V_FW + KF * k + made + e), 1)])\
                            .then_inc(conv_out, 1)
                    split(l, T_UP[g] // 2 + 2, q)
                    for e in range(2):
                        dve.wait_ge(tile_done, l * TL + q * 4 + (T_UP[g] + 2 + e + 5))
                        dve.wait_ge(gelu_out, l * KF + q * 2 + (made + e + 1))
                        product(HID[e], pp(GE[e]), sp4(GE[e]), slot(v_slot + e), psum_free[e])
                        dve.wait_ge(prod_hi, l * 30 + q * 2 + (8 + made + e + 1))
                        mid = bass.ds(q * 2 + e, 1)
                        low(ML[:, mid].rearrange("p o h n -> p (o h) n"), halves(HID[e]),
                            MH[:, mid].rearrange("p o h n -> p (o h) n"), mid_ready)

                made = 0
                for g, K in enumerate(GROUPS):
                    base, at, first = step.base, step.n, 0
                    if g == 0:
                        up_quad(0, 0, 0, 2)
                        first = 1
                        assert step.n == at + UP_STEPS
                    with dve.Fori(first, K // 2) as q:
                        step.base, step.n = base + at + q * UP_STEPS, 0
                        up_quad(g, q, made, 0)
                        assert step.n == UP_STEPS, step.n
                    step.base, step.n = base, at + UP_STEPS * (K // 2)
                    if g == 0:
                        modulation(l * 3 + 4, MOD_SH1, BNEXT[:])
                    nd = T_DN[g] // 2
                    if g < 2:
                        base, at = step.base, step.n
                        with dve.Fori(0, 2) as q:
                            step.base, step.n = base + at + q * 4, 0
                            for e in range(4):
                                if e % 2 == 0:
                                    split(l, nd + 1 + e // 2, q)
                                residual(l * TL + q * 4 + (T_DN[g] + e + 5), e % 2,
                                         X[:, bass.ds(q * 4 + e, 1)].rearrange("p o h n -> p (o h) n"),
                                         lambda a_, b_, e=e: MOD[:, bass.ds(q * 4 + (MOD_G2 + e), 1), a_:b_]
                                         .rearrange("p o j -> p (o j)"),
                                         l * PL + q * 2 + (T_DN[g] // 2 + e // 2 + 2))
                            assert step.n == 4
                        step.base, step.n = base, at + 8
                    else:
                        V.tensor_copy(XTMP[:, 0, 0:1], NS[:, 0:1]).then_inc(ns_ready, 1)
                        dve.wait_ge(ns_ready, l + 1)
                        split(l, nd + 1)
                        step(V.tensor_copy(CUR[:], VEC[:, bass.ds(after, 1), :].rearrange("p o n -> p (o n)")))
                        dve.wait_ge(mod_ready, l * 3 + 4)
                        gains(MOD_SC1, V_N1)
                        for m in range(KX):
                            residual(done(l, T_DN[g] + m), m % 2, X[:, m], lambda a_, b_, m=m: MOD[:, MOD_G2 + m, a_:b_],
                                     read(l, T_DN[g] + m), x_ready)
                            if m:
                                sum_square(l * 16 + 16, m - 1)
                            if m in (1, 3):
                                split(l, nd + 2 + m // 2)
                            if m == 5:
                                split(l, PL)
                        sum_square(l * 16 + 16, KX - 1)
                        rstd(l * 2 + 3)
                    made += K
                assert step.n == DVE_STEPS, step.n
            step.base, step.n = L * DVE_STEPS + before, 0
            dve.wait_ge(fg_in, 16)
            for i, h, t0, w in token_tiles():
                s = i % 3
                dve.wait_ge(y_cols, i + 1)
                V.scalar_tensor_tensor(out=YROW[i][0:w].rearrange("p (b n) -> p b n", b=2), in0=PS[0:w, 2 * s:2 * s + 2, :],
                                       scalar=RST[0:w, i:i + 1], in1=FGB[0:w].rearrange("p (b n) -> p b n", b=2),
                                       op0=ALU.mult, op1=ALU.mult).then_inc(y_rows, 1)


UP_STEPS = 6
DVE_STEPS = 180

_OUT = ["y_prompt", "y_sample", "new_lru_h_p", "new_lru_conv_p", "new_sc_conv_p", "new_ffn_conv_p",
        "new_lru_h_s", "new_lru_conv_s", "new_sc_conv_s", "new_ffn_conv_s"]
_INS = ["x_prompt", "x_sample", "c_prompt", "c_sample", "state_lru_h", "state_lru_conv", "state_sc_conv",
        "state_ffn_conv", "w_ada", "b_ada", "norm1_g", "norm2_g", "w_in", "lru_conv_w", "lru_conv_b", "lru_wa",
        "lru_ba", "lru_wx", "lru_bx", "lru_lambda", "sc_conv_w", "w_out", "ffn_w_up", "ffn_conv_w", "ffn_w_down",
        "final_g"]


def kernel(**inputs):
    import numpy as np
    import concourse.bacc as bacc
    from concourse.bass_utils import run_bass_kernel_spmd

    nc = bacc.Bacc("TRN2", target_bir_lowering=False, num_devices=1)
    arrays, a, o = {}, {}, {}
    for name in _INS:
        arrays["in_" + name] = x = np.ascontiguousarray(inputs[name])
        a[name] = nc.dram_tensor("in_" + name, x.shape, mybir.dt.from_np(x.dtype), kind="ExternalInput").ap()
    L, DB, _, DH = inputs["state_lru_conv"].shape
    DFF = inputs["state_ffn_conv"].shape[3]
    shapes = [inputs["x_prompt"].shape, inputs["x_sample"].shape]
    for b in (1, DB):
        shapes += [(L, b, DH), (L, b, 3, DH), (L, b, 2, DH), (L, b, 2, DFF)]
    for name, shape in zip(_OUT, shapes):
        o[name] = nc.dram_tensor("out_" + name, tuple(shape), F32, kind="ExternalOutput").ap()
    hybrid_trunk_kernel(nc, a, o)
    r = run_bass_kernel_spmd(nc, [arrays], core_ids=[0])
    return tuple(r.results[0]["out_" + name] for name in _OUT)
```

```python
from contextlib import ExitStack

import concourse.bass as bass
from concourse import mybir

F32 = mybir.dt.float32
F32R = mybir.dt.float32r
ALU = mybir.AluOpType
ACT = mybir.ActivationFunctionType
P = 128
EPS = 1e-6
RG_C = 8.0


def hybrid_trunk_kernel(nc, a, o):
    L, D = a["w_ada"].shape[:2]
    SEQ = a["x_prompt"].shape[1]
    NB, TS = a["x_sample"].shape[:2]
    DH = a["lru_lambda"].shape[1]
    DFF = a["ffn_conv_w"].shape[2]
    HD = a["lru_wa"].shape[2]
    KX, KH, KF = D // P, DH // P, DFF // P
    HALF = (SEQ + NB * TS) // 2
    HP, HB = SEQ // 2, NB // 2
    HS = HALF - HP
    TOK = 2 * HALF
    PADS = 3
    SB0, SW = PADS + SEQ, PADS + TS
    PADW = SB0 + NB * SW
    NJ = 1 + NB
    GROUPS = [8, 8, KF - 16]
    NST_ = NB * TS
    assert (L, KX, KH, KF, HALF, NJ) == (2, 8, 4, 22, 288, 9)

    V_BADA, V_N1, V_N2, V_CW, V_CB, V_BA, V_BX, V_LAM, V_SW = 0, 48, 56, 64, 80, 84, 88, 92, 96
    V_FW, V_SH, V_SLC, V_SSC, V_SF, V_SP, V_NSP, VN = 108, 174, 206, 302, 366, 718, 722, 726
    VT = [(0, 108, 4, 0), (1, 98, 4, 108), (2, 96, 4, 206), (3, 64, 4, 302),
          (4, 128, 5, 0), (5, 128, 5, 128), (6, 96, 5, 256)]
    N_LCS, N_SCS, N_HS, N_LCP, N_SCP, N_HP, N_FP, N_FS, NN = 0, 96, 160, 192, 204, 212, 216, 260, 612
    NST = [(0, 96), (96, 96), (192, 68), (260, 128), (388, 128), (516, 96)]
    NSO = [("lru_conv_s", 0, 0, 96, 0), ("sc_conv_s", 1, 0, 64, 0), ("lru_h_s", 1, 64, 32, 0),
           ("lru_conv_p", 2, 0, 12, 0), ("sc_conv_p", 2, 12, 8, 0), ("lru_h_p", 2, 20, 4, 0),
           ("ffn_conv_p", 2, 24, 44, 0), ("ffn_conv_s", 3, 0, 128, 0), ("ffn_conv_s", 4, 0, 128, 128),
           ("ffn_conv_s", 5, 0, 96, 256)]

    T_CS, T_HS, T_BS, T_GL, T_WOUT = 4, 8, 12, 16, 20
    T_UP, T_DN = [28, 52, 76], [44, 68, 88]
    SIDE = 2
    TL, PL = 96, 48
    MOD_SH1, MOD_G1, MOD_SH2, MOD_SC2, MOD_G2 = 0, 16, 24, 32, 40
    MOD_SC1 = 8

    with ExitStack() as ctx:
        def sb(name, shape, dt=F32):
            return ctx.enter_context(nc.sbuf_tensor(name, shape, dt))

        def sem(name):
            return ctx.enter_context(nc.semaphore(name))

        X = sb("X", [P, KX, 2, HALF])
        NH = sb("norm_hi", [P, KX, 2, HALF], F32R)
        NL = sb("norm_lo", [P, KX, 2, HALF], F32R)
        MH = sb("mid_hi", [P, 8, 2, HALF], F32R)
        ML = sb("mid_lo", [P, 8, 2, HALF], F32R)
        RAW = sb("w_raw", [P, 2, 8, 256])
        WH = sb("w_hi", [P, 2, 8, 256], F32R)
        WL = sb("w_lo", [P, 2, 8, 256], F32R)
        AW = sb("ada_w", [P, 2048])
        CT = sb("silu_c", [P, KX, 32])
        VEC = sb("vec", [P, L, VN])
        CUR = sb("vec_now", [P, VN])
        MOD = sb("mod", [P, 6 * KX, NJ])
        GS = sb("gain", [P, KX, NJ])
        BNEXT = sb("bias_next", [P, 16])
        ADS = sb("ada_rows", [P, 512])
        BLK = sb("gate_w", [P, 2, KH, P])
        IDN = sb("ident", [P, P])
        ONE = sb("ones", [P, P])
        AVG = sb("avg", [P, 1])
        EPST = sb("eps", [P, 1])
        STD = sb("std", [P, 6])
        RST = sb("rstd", [P, 6])
        NS = sb("new_states", [P, NN])
        SMALL = sb("small", [P, 160])
        XTMP = sb("x_tmp", [P, 2, NST_])
        WORK = sb("work", [P, 15 * PADW])

        def wk(i):
            return WORK[:, i * PADW:(i + 1) * PADW]

        CIN = [wk(0), wk(1)]
        XC = [wk(2 + c) for c in range(KH)]
        Z = [wk(6 + c) for c in range(KH)]
        TR, TI, TT = wk(10), wk(11), wk(12)
        HID = [wk(13), wk(14)]
        UC, GE = [wk(2), wk(3)], [wk(4), wk(5)]
        ACC = wk(14)[:, 0:TOK]
        SQ = [wk(11)[:, 0:TOK], wk(12)[:, 0:TOK]]
        SQ0 = [NS[:, 0:TOK], CUR[:, 0:TOK]]
        RSS = wk(4)[:, 0:TOK]
        T1 = [wk(3)[:, 0:TOK], wk(5)[:, 0:TOK]]
        DIAG = WORK[:, 13 * PADW:13 * PADW + 6 * P].rearrange("p (i n) -> p i n", i=6)
        NSR = WORK[:, 7 * PADW:7 * PADW + 6 * P].rearrange("p (i n) -> p i n", i=6)
        FGB = WORK[:, 0:D]
        XROW = WORK[:, 0:6 * D].rearrange("p (a n) -> p a n", a=6)
        VROW = WORK[:, 6 * D:6 * D + 15 * P].rearrange("p (a n) -> p a n", a=15)
        RAWF = [RAW[:, i].rearrange("p k n -> p (k n)") for i in range(2)]
        EARLY = [(AW[:], None), (RAWF[0], None), (RAWF[1], None), (WORK[:, 0:2048], None), (WORK[:, 2048:4096], None),
                 (WORK[:, 4096:6144], None), (AW[:], 0), (WORK[:, 0:2048], 3)]
        YROW = [RAW[:, i // 2].rearrange("p k n -> p (k n)")[:, (i % 2) * D:(i % 2 + 1) * D] for i in range(4)] \
            + [AW[:, 0:D], AW[:, D:2 * D]]

        PS = ctx.enter_context(nc.psum_tensor("ps", [P, 8, 512], F32))
        B_R, B_I, B_MISC, B_ADA = 4, 5, 6, 7

        def halves(t):
            return t[:, 0:TOK].rearrange("p (h n) -> p h n", h=2)

        def pr(t3):
            return t3[:, :, 0:HP]

        def sm(t3):
            return t3[:, :, HP:HALF].rearrange("p h (b t) -> p h b t", t=TS)

        def pp(t):
            return t[:, PADS:SB0].rearrange("p (h n) -> p h n", h=2)

        def spad(t):
            return t[:, SB0:PADW].rearrange("p (b n) -> p b n", b=NB)

        def sp4(t):
            return t[:, SB0:PADW].rearrange("p (h b n) -> p h b n", h=2, b=HB)[:, :, :, PADS:SW]

        def slot(s):
            return PS[:, 2 * s:2 * s + 2, 0:HALF]

        def perseq(v):
            return v.rearrange("p (h b u) -> p h b u", h=2, u=1).broadcast_to([P, 2, HB, TS])

        def token_tiles():
            return [(i, i // 2, (i % 2) * P, P) if i < 4 else (i, i - 4, HP, HS) for i in range(6)]

        def half_tiles(h):
            return [(t0, w, 3 * h + t0 // P) for _, hh, t0, w in token_tiles() if hh == h]

        def turned(i):
            return PS[:, 2 * (i % 3):2 * (i % 3) + 2, :].rearrange("p b (q n) -> p (b q) n", n=P)

        def stat_bank(h):
            return PS[:, B_ADA if h else B_I, 400:406]

        tile_done = sem("tile_done")
        half_done, norm_p = sem("half_done"), sem("norm_p")
        hi_half, lo_half = sem("hi_half"), sem("lo_half")
        psum_free = [sem("psum_free0"), sem("psum_free1")]
        raw_full = [sem("raw_full0"), sem("raw_full1")]
        hi_done, lo_done = sem("hi_done"), sem("lo_done")
        ada_w_full, ada_slices = sem("ada_w_full"), sem("ada_slices")
        ada_rows_ready, ada_cols_done, mod_ready = sem("ada_rows_ready"), sem("ada_cols_done"), sem("mod_ready")
        blk_full, gate_done, gate_read, xc_ready = sem("blk_full"), sem("gate_done"), sem("gate_read"), sem("xc_ready")
        lru_act, m2_ready, scan_ready = sem("lru_act"), sem("m2_ready"), sem("scan_ready")
        conv_out, gelu_out = sem("conv_out"), sem("gelu_out")
        lru_prod, prod_hi, mid_ready = sem("lru_prod"), sem("prod_hi"), sem("mid_ready")
        norm_f, norm_hi, norm_ready = sem("norm_f"), sem("norm_hi_ready"), sem("norm_ready")
        x_ready, sq_ready, acc_ready = sem("x_ready"), sem("sq_ready"), sem("acc_ready")
        stat_done, std_ready, diag_ready, rs_done = sem("stat_done"), sem("std_ready"), sem("diag_ready"), sem("rs_done")
        ns_ready, ns_rows, ns_out, ns_stored = sem("ns_ready"), sem("ns_rows"), sem("ns_out"), sem("ns_stored")
        dve_step, act_step, pool_step = sem("dve_step"), sem("act_step"), sem("pool_step")
        c_in, ident_ready = sem("c_in"), sem("ident_ready")
        x_in = [sem(f"x_in{i}") for i in range(6)]
        c_cols, c_sig, c_ready, v_cols, v_ready = sem("c_cols"), sem("c_sig"), sem("c_ready"), sem("v_cols"), sem("v_ready")
        x_cols, lam_e = sem("x_cols"), sem("lam_e")
        x_copied, x_moved = sem("x_copied"), sem("x_moved")
        fg_in, y_cols, y_rows, y_out = sem("fg_in"), sem("y_cols"), sem("y_rows"), sem("y_out")
        early_full = [sem(f"early_full{k}") for k in range(KX)]
        v_in = [sem(f"v_in{l}") for l in range(L)]
        t1_ready, rs_copied, ns_read = sem("t1_ready"), sem("rs_copied"), sem("ns_read")
        NVEC = 16

        block = ctx.enter_context(nc.Block())

        def done(l, t):
            return l * TL + t + 5

        def read(l, t):
            return l * (TL // 2) + t // 2 + 2

        def vectors(engine, l, part=slice(None)):
            def rows(name):
                return a[name][l].rearrange("(k p) -> k p", p=P)
            fs = a["state_ffn_conv"][l].rearrange("b k (c p) -> (b k c) p", p=P)
            for i, r, src in (
                    (0, V_BADA, rows("b_ada")), (0, V_N1, rows("norm1_g")), (0, V_N2, rows("norm2_g")),
                    (0, V_CW, a["lru_conv_w"][l].rearrange("k (c p) -> (k c) p", p=P)),
                    (0, V_CB, rows("lru_conv_b")), (0, V_BA, rows("lru_ba")), (0, V_BX, rows("lru_bx")),
                    (0, V_LAM, rows("lru_lambda")),
                    (0, V_SW, a["sc_conv_w"][l].rearrange("k (c p) -> (k c) p", p=P)),
                    (1, 0, a["ffn_conv_w"][l].rearrange("k (c p) -> (k c) p", p=P)),
                    (1, V_SH - V_FW, a["state_lru_h"][l].rearrange("b (c p) -> (b c) p", p=P)),
                    (2, 0, a["state_lru_conv"][l].rearrange("b k (c p) -> (b k c) p", p=P)),
                    (3, 0, a["state_sc_conv"][l].rearrange("b k (c p) -> (b k c) p", p=P)),
                    (4, 0, fs[0:128]), (5, 0, fs[128:256]), (6, 0, fs[256:352]))[part]:
                engine.dma_start(VROW[r:r + src.shape[0], 7 * l + i, :], src).then_inc(v_in[l], 16)

        @block.sync
        def _(sp):
            for r, src in ((0, a["c_prompt"]), (8, a["c_sample"])):
                src = src.rearrange("b (k p) -> (b k) p", p=P)
                sp.dma_start(VROW[r:r + src.shape[0], 14, :], src).then_inc(c_in, 16)
            xs = a["x_sample"].rearrange("b t n -> (b t) n")
            for i, h, t0, w in token_tiles():
                src = a["x_prompt"][0, i * P:(i + 1) * P, :] if i < 4 else xs[h * HS:(h + 1) * HS, :]
                sp.dma_start(XROW[0:w, i, :], src).then_inc(x_in[i], 16)

            def load(p, s, src):
                src = src.rearrange("o (k p) c -> p (o k) c", p=P)
                sp.wait_ge(lo_done, p + 1)
                sp.dma_start(RAW[:, s, 0:src.shape[1], :], src).then_inc(raw_full[s], 16)

            ada0 = a["w_ada"][0].rearrange("(k p) c -> k p c", p=P)
            for k, (dst, after) in enumerate(EARLY):
                if k == 3:
                    vectors(sp, 0, slice(8, None))
                    sp.wait_ge(x_cols, 6)
                if k == KX - 1:
                    sp.wait_ge(ada_slices, 4)
                    load(0, 0, a["w_in"][0:1, :, 0:256])
                if after is not None:
                    sp.wait_ge(ada_slices, after + 2)
                sp.dma_start(dst, ada0[k, :, 0:2048]).then_inc(early_full[k], 16)

            with sp.Fori(0, L) as l:
                load(l * PL + 1, 1, a["w_in"][bass.ds(l, 1), :, 256:512])
                n = 2
                for c0 in (3 * DH, 4 * DH, 2 * DH, DH):
                    for s in range(2):
                        load(l * PL + n, s, a["w_in"][bass.ds(l, 1), :, c0 + 256 * s:c0 + 256 * s + 256])
                        n += 1
                for j in range(4):
                    load(l * PL + n, j % 2, a["w_out"][bass.ds(l, 1), :, 256 * j:256 * j + 256])
                    n += 1
                for g, K in enumerate(GROUPS):
                    with sp.Fori(0, K // 2) as q:
                        for s in range(2):
                            load(l * PL + q * 2 + (n + s), s,
                                 a["ffn_w_up"][bass.ds(l, 1), :, bass.ds(q * 256 + (8 * g * P + s * DFF), 256)])
                    n += K
                    for j in range(4):
                        load(l * PL + n, j % 2,
                             a["ffn_w_down"][bass.ds(l, 1), 8 * g * P:(8 * g + K) * P, 256 * j:256 * j + 256])
                        n += 1
                assert n == PL
                after = l * -1 + (L - 1)
                load(l * PL + n, 0, a["w_in"][bass.ds(after, 1), :, 0:256])
            sp.wait_ge(lo_done, L * PL + 3)
            sp.dma_start(FGB, a["final_g"].rearrange("(u n) -> u n", u=1).broadcast_to([P, D])).then_inc(fg_in, 16)
            ys = o["y_sample"].rearrange("b t n -> (b t) n")
            for i, h, t0, w in token_tiles():
                sp.wait_ge(y_rows, i + 1)
                dst = o["y_prompt"][0, i * P:(i + 1) * P, :] if i < 4 else ys[h * HS:(h + 1) * HS, :]
                sp.dma_start(dst, YROW[i][0:w, :]).then_inc(y_out, 16)
            sp.wait_ge(y_out, 16 * 6)

        @block.gpsimd
        def _(pool):
            pool.sem_inc(ns_stored, 1)
            nc.gpsimd.memset(IDN[:], 0.0).then_inc(pool_step, 1)
            pool.wait_ge(pool_step, 1)
            nc.gpsimd.affine_select(out=IDN[:], in_=IDN[:], compare_op=ALU.not_equal, fill=1.0, base=0,
                                    pattern=[[-1, P]], channel_multiplier=1).then_inc(ident_ready, 1)
            nc.gpsimd.memset(ONE[:], 1.0).then_inc(ident_ready, 1)
            nc.gpsimd.memset(AVG[:], 1.0 / D).then_inc(ident_ready, 1)
            nc.gpsimd.memset(EPST[:], EPS).then_inc(ident_ready, 1)
            for l in range(1, L):
                vectors(pool, l)
            nc.gpsimd.memset(BLK[:], 0.0).then_inc(pool_step, 1)

            def ada_load(n, l, r, k):
                chunk = l * KX + k
                pool.wait_ge(ada_slices, n + 1)
                pool.dma_start(AW[:], a["w_ada"].rearrange("l (k p) c -> (l k) p c", p=P)
                               [bass.ds(chunk, 1), :, r * 2048:(r + 1) * 2048]
                               .rearrange("o p c -> p (o c)")).then_inc(ada_w_full, 16)

            pool.wait_ge(pool_step, 2)
            pool.wait_ge(early_full[KX - 1], 16)
            with pool.Fori(0, L) as l:
                pool.wait_ge(gate_done, l * 8 + 1)
                for m, w in enumerate(("lru_wa", "lru_wx")):
                    for q in range(2):
                        src = a[w][bass.ds(l, 1)].rearrange("o (c q) i j -> q i (o c) j", q=2)[q]
                        pool.dma_start(BLK[q * HD:(q + 1) * HD, m, :, q * HD:(q + 1) * HD], src).then_inc(blk_full, 16)
                after = l * -1 + (L - 1)
                for i, (lr, r) in enumerate(((l, 1), (l, 2), (after, 0))):
                    with pool.Fori(0, KX) as k:
                        ada_load(l * 24 + k + (8 + 8 * i), lr, r, k)
                pool.wait_ge(ns_read, l * 6 + 6)
                for name, i, r, n, r0 in NSO:
                    dst = o["new_" + name][bass.ds(l, 1)]
                    dst = dst.rearrange("o b (c p) -> (o b c) p", p=P) if len(dst.shape) == 3 else \
                        dst.rearrange("o b k (c p) -> (o b k c) p", p=P)
                    pool.dma_start(dst[r0:r0 + n], NSR[r:r + n, i, :]).then_inc(ns_out, 16)
                pool.wait_ge(ns_out, l * (16 * len(NSO)) + 16 * len(NSO))
                pool.sem_inc(ns_stored, 1)

        @block.tensor
        def _(pe):
            T = nc.tensor
            pe.sem_inc(tile_done, 4)
            pe.sem_inc(ada_slices, 1)
            pe.sem_inc(gate_done, 1)

            def chunk(i, s, k, xh, xl, start, stop):
                r, c = i // 2, (i % 2) * P
                for h in range(2):
                    out = PS[:, 2 * s + h, 0:HALF]
                    T.matmul(out, WH[:, r, k, c:c + P], xh[:, k, h, :], start=start, stop=False)
                    T.matmul(out, WH[:, r, k, c:c + P], xl[:, k, h, :], start=False, stop=False)
                    last = T.matmul(out, WL[:, r, k, c:c + P], xh[:, k, h, :], start=False, stop=stop)
                return last

            def tile(pair, i, xh, xl, order, ready=None):
                if i % 2 == 0:
                    pe.wait_ge(lo_done, pair + (i // 2 + 3))
                pe.wait_ge(psum_free[i % 2], pair + (i // 2 + 1))
                for j, k in enumerate(order):
                    if ready is not None:
                        pe.wait_ge(ready[0], ready[1] + (j + 1))
                    last = chunk(i, i % 2, k, xh, xl, j == 0, j == len(order) - 1)
                last.then_inc(tile_done, 1)

            def last_tile(pair, order):
                pe.wait_ge(psum_free[1], pair + 2)
                for h in range(2):
                    out = PS[:, 2 + h, 0:HALF]
                    for j, k in enumerate(order):
                        hi, lo = WH[:, 1, k, P:2 * P], WL[:, 1, k, P:2 * P]
                        T.matmul(out, hi, MH[:, k, h, :], start=(j == 0), stop=False)
                        T.matmul(out, hi, ML[:, k, h, :], start=False, stop=False)
                        last = T.matmul(out, lo, MH[:, k, h, :], start=False, stop=(j == len(order) - 1))
                    last.then_inc(tile_done if h else half_done, 1)

            def first_quad(pair, ready, rs):
                for k, tiles in [(k, range(4)) for k in range(SIDE)] + \
                        [(k, t) for t in ((0, 1), (2, 3)) for k in range(SIDE, KX)]:
                    if 0 in tiles:
                        pe.wait_ge(norm_ready, ready + (k + 1))
                    if k == KX // 2 and 2 in tiles:
                        pe.wait_ge(lo_done, pair + 4)
                    for i in tiles:
                        if k == 0:
                            if i == 0:
                                pe.wait_ge(lo_done, pair + 3)
                            if i == 2:
                                pe.wait_ge(lo_half, rs)
                            if i < 2:
                                pe.wait_ge(psum_free[i], pair + 1)
                            if i == 3:
                                pe.wait_ge(rs_copied, rs)
                        last = chunk(i, i, k, NH, NL, k == 0, k == KX - 1)
                        if k == KX - 1:
                            last.then_inc(tile_done, 1)

            def ada_slice(n, k):
                src = EARLY[k][0] if n is None else AW
                if n is None:
                    pe.wait_ge(early_full[k], 16)
                else:
                    pe.wait_ge(ada_w_full, (n - KX) * 16 + 16)
                for g in range(4):
                    last = T.matmul(PS[32 * g:32 * g + 32, B_ADA, :], CT[:, k, :], src[:, g * 512:(g + 1) * 512],
                                    start=(k == 0), stop=(k == KX - 1))
                last.then_inc(ada_slices, 1)

            def ada_turn(m):
                pe.wait_ge(ada_rows_ready, m)
                for q in range(4):
                    last = T.transpose(PS[:, B_MISC, q * P:(q + 1) * P], ADS[:, q * P:(q + 1) * P], IDN[:])
                last.then_inc(ada_cols_done, 1)

            def norm_stats(m, h):
                pe.wait_ge(acc_ready, m * 2 + (h - 1))
                for t0, w, c in half_tiles(h):
                    last = T.matmul(stat_bank(h)[0:w, c:c + 1], ACC[:, h * HALF + t0:h * HALF + t0 + w], AVG[:],
                                    start=True, stop=True)
                last.then_inc(stat_done, 1)

            def norm_spread(m, h):
                pe.wait_ge(diag_ready, m * 2 + (h - 1))
                for t0, w, c in half_tiles(h):
                    last = T.matmul(PS[:, 6 + h, t0:t0 + w], ONE[0:w, :], DIAG[0:w, c, 0:w], start=True, stop=True)
                last.then_inc(rs_done, 1)

            pe.wait_ge(ident_ready, 4)
            pe.wait_ge(c_in, 32)
            T.transpose(PS[:, B_MISC, 0:72], VROW[0:72, 14, :], IDN[0:72, 0:72]).then_inc(c_cols, 1)
            for i, h, t0, w in token_tiles():
                pe.wait_ge(x_in[i], 16)
                if i >= 3:
                    pe.wait_ge(x_copied if i % 2 == 0 else x_moved, i // 2)
                for k in range(KX):
                    last = T.transpose(turned(i)[:, k, 0:w], XROW[0:w, i, k * P:(k + 1) * P], IDN[0:w, 0:w])
                last.then_inc(x_cols, 1)
            for h in range(2):
                norm_stats(1, h)
            pe.wait_ge(c_ready, 1)
            pe.wait_ge(std_ready, 2)
            for k in range(KX):
                ada_slice(None, k)
                if k == 2:
                    for l in range(L):
                        pe.wait_ge(v_in[l], 16 * NVEC)
                        if l == 0:
                            pe.wait_ge(x_copied, 3)
                            pe.wait_ge(x_moved, 3)
                        for i, n, b, c in VT:
                            last = T.transpose(PS[:, b - 4 * l, c:c + n], VROW[0:n, 7 * l + i, :], IDN[0:n, 0:n])
                        last.then_inc(v_cols, 1)
            ada_turn(1)

            with pe.Fori(0, L) as l:
                pe.wait_ge(mod_ready, l * 3 + 1)
                for h in range(2):
                    norm_spread(l * 2 + 1, h)
                first_quad(l * PL, l * 16, l * 2 + 1)
                for t in range(4, T_UP[0]):
                    if t < T_WOUT:
                        tile(l * PL + t // 4 * 2, t % 4, NH, NL, range(KX))
                    elif t == T_UP[0] - 1:
                        last_tile(l * PL + t // 4 * 2, range(KX))
                    else:
                        tile(l * PL + t // 4 * 2, t % 4, MH, ML, [4, 5, 6, 7, 0, 1, 2, 3],
                             (mid_ready, l * 30) if t == T_WOUT else None)
                    if t in (12, 20):
                        if t == 12:
                            pe.wait_ge(gate_read, l * 8 + 4)
                        ada_turn(l * 3 + (2 if t == 12 else 3))
                    i, k = (t - 4) // 8, (t - 4) % 8
                    if t == 4:
                        pe.wait_ge(psum_free[1], l * PL + 3)
                    if k == 0:
                        pe.wait_ge(ada_rows_ready, l * 3 + (i + 1))
                    ada_slice(l * 24 + (8 + 8 * i + k), k)
                    if t in (9, 11, 13, 15):
                        c = (t - 9) // 2
                        pe.wait_ge(xc_ready, l * 4 + (c + 1))
                        if c == 0:
                            pe.wait_ge(blk_full, l * 64 + 64)
                        else:
                            if c == 2:
                                pe.wait_ge(mod_ready, l * 3 + 2)
                            pe.wait_ge(gate_read, l * 8 + 2 * c)
                        for m, b in ((0, B_R), (1, B_I)):
                            T.matmul(PS[:, b, :], BLK[:, m, c, :], XC[c][:, PADS:SB0], start=True, stop=True)
                            T.matmul(PS[:, B_MISC, m * NST_:(m + 1) * NST_], BLK[:, m, c, :],
                                     spad(XC[c])[:, :, PADS:SW], start=True, stop=True).then_inc(gate_done, 1)
                pe.wait_ge(gate_read, l * 8 + 8)
                norm_stats(l * 2 + 2, 0)
                pe.wait_ge(ada_rows_ready, l * 3 + 4)
                norm_stats(l * 2 + 2, 1)
                pe.wait_ge(mod_ready, l * 3 + 3)
                for h in range(2):
                    norm_spread(l * 2 + 2, h)
                first_quad(l * PL + T_UP[0] // 2, l * 16 + 8, l * 2 + 2)
                made = 8
                for g, K in enumerate(GROUPS):
                    with pe.Fori(1 if g == 0 else 0, K // 2) as q:
                        for i in range(4):
                            tile(l * PL + q * 2 + T_UP[g] // 2, i, NH, NL, range(KX))
                    if g == 0:
                        ada_turn(l * 3 + 4)
                    with pe.Fori(0, 2 if g < 2 else 1) as q:
                        for i in range(4):
                            tile(l * PL + q * 2 + T_DN[g] // 2, i, MH, ML, range(K),
                                 (mid_ready, l * 30 + made) if i == 0 else None)
                    if g == 2:
                        pe.wait_ge(ns_ready, l + 1)
                        pe.wait_ge(mod_ready, l * 3 + 4)
                        for i, (c0, n) in enumerate(NST):
                            last = T.transpose(PS[0:n, B_MISC if i < 4 else B_R, (i % 4) * P:(i % 4 + 1) * P],
                                               NS[:, c0:c0 + n], IDN[:])
                        last.then_inc(ns_rows, 1)
                        for i in range(3):
                            tile(l * PL + T_DN[g] // 2 + 2, i, MH, ML, range(K))
                        last_tile(l * PL + T_DN[g] // 2 + 2, range(K))
                    made += K
                pe.wait_ge(ns_read, l * 6 + 6)
                for h in range(2):
                    norm_stats(l * 2 + 3, h)
            for i, h, t0, w in token_tiles():
                s = i % 3
                if i == 2:
                    pe.wait_ge(std_ready, 2 * (2 * L + 1))
                if i >= 3:
                    pe.wait_ge(y_rows, i - 2)
                for k in range(KX):
                    last = T.transpose(PS[0:w, 2 * s + k // 4, (k % 4) * P:(k % 4 + 1) * P], X[:, k, h, t0:t0 + w], IDN[:])
                last.then_inc(y_cols, 1)

        @block.scalar
        def _(act):
            A = nc.scalar.activation
            vectors(act, 0, slice(0, 8))

            def split(l, n, q=0):
                s = n % 2
                act.wait_ge(raw_full[s], l * (8 * PL) + q * 16 + 16 * (n // 2 + 1))
                act.wait_ge(tile_done, l * TL + q * 4 + (2 * n + 2))
                A(WH[:, s], RAW[:, s], ACT.Copy).then_inc(hi_done, 1)

            def split_halves(l, n):
                s = n % 2
                act.wait_ge(raw_full[s], l * (8 * PL) + 16 * (n // 2 + 1))
                act.wait_ge(tile_done, l * TL + (2 * n + 2))
                A(WH[:, s, 0:KX // 2], RAW[:, s, 0:KX // 2], ACT.Copy).then_inc(hi_half, 1)
                A(WH[:, s, KX // 2:KX], RAW[:, s, KX // 2:KX], ACT.Copy).then_inc(hi_done, 1)

            def ada_rows(m, first=False):
                act.wait_ge(ada_slices, m * 8 + 1)
                if not first:
                    act.wait_ge(ada_cols_done, m - 1)
                A(ADS[:], PS[:, B_ADA, :], ACT.Copy).then_inc(ada_rows_ready, 1)

            def std(m):
                for h in range(2):
                    act.wait_ge(stat_done, m * 2 + (h - 1))
                    A(STD[:, 3 * h:3 * h + 2], stat_bank(h)[:, 3 * h:3 * h + 2], ACT.Sqrt, bias=EPST[:])
                    A(STD[0:HS, 3 * h + 2:3 * h + 3], stat_bank(h)[0:HS, 3 * h + 2:3 * h + 3], ACT.Sqrt,
                      bias=EPST[0:HS, :]).then_inc(std_ready, 1)

            def square(n, m):
                act.wait_ge(x_ready, n + (m + 1))
                if m < KX - 1:
                    A(halves(SQ[m % 2]), X[:, m], ACT.Square).then_inc(sq_ready, 1)
                else:
                    h = m - (KX - 1)
                    A(halves(SQ[1])[:, h], X[:, KX - 1, h], ACT.Square).then_inc(sq_ready, 1)

            def norm_round(m, n, sh):
                for k in range(KX):
                    act.wait_ge(t1_ready, n + (k + 1))
                    if k == 1:
                        A(halves(RSS), PS[:, 6:8, 0:HALF], ACT.Copy).then_inc(rs_copied, 1)
                    if k >= 2:
                        act.wait_ge(norm_ready, n + (k - 1))
                    A(pr(halves(HID[k % 2])), pr(halves(T1[k % 2])), ACT.Identity, scale=GS[:, k, 0:1],
                      bias=MOD[:, sh + k, 0:1]).then_inc(norm_p, 1)
                    act.wait_ge(norm_p, n + (k + 1))
                    act.wait_ge(norm_f, n + (k + 1))
                    A(NH[:, k], halves(HID[k % 2]), ACT.Copy).then_inc(norm_hi, 1)

            act.wait_ge(c_cols, 1)
            A(SMALL[:, 0:72], PS[:, B_MISC, 0:72], ACT.Sigmoid).then_inc(c_sig, 1)
            act.preload_act_table(ACT.Sqrt)
            for i, h, t0, w in token_tiles():
                if i % 2:
                    act.wait_ge(x_cols, i + 1)
                    A(X[:, :, h, t0:t0 + w], turned(i)[:, :, 0:w], ACT.Copy).then_inc(x_copied, 1)
            act.wait_ge(x_copied, 3)
            act.wait_ge(x_moved, 3)
            for k in range(KX):
                if k >= 2:
                    act.wait_ge(dve_step, k + 2)
                A(halves(SQ0[k % 2]), X[:, k], ACT.Square).then_inc(sq_ready, 1)
            std(1)
            for l in range(L):
                act.wait_ge(v_cols, l + 1)
                A(VEC[:, l, 0:366], PS[:, 4 - 4 * l, 0:366], ACT.Copy).then_inc(v_ready, 1)
                A(VEC[:, l, 366:718], PS[:, 5 - 4 * l, 0:352], ACT.Copy).then_inc(v_ready, 1)
            act.wait_ge(v_ready, 2 * L)
            for l in range(L):
                A(SMALL[:, 80 + 4 * l:84 + 4 * l], VEC[:, l, V_LAM:V_LAM + 4], ACT.Abs).then_inc(act_step, 1)
            act.wait_ge(act_step, L)
            A(SMALL[:, 88:96], SMALL[:, 80:88], ACT.Exp, scale=-1.0).then_inc(lam_e, 1)
            act.preload_act_table(ACT.Sqrt)
            split(0, 0)
            ada_rows(1, first=True)

            with act.Fori(0, L) as l:
                split_halves(l, 1)
                norm_round(l * 2 + 1, l * 16, MOD_SH1)
                for c in range(KH):
                    act.wait_ge(tile_done, done(l, c))
                    if c >= 2:
                        act.wait_ge(xc_ready, l * 4 + (c - 1))
                    A(pp(CIN[c % 2]), pr(slot(c)), ACT.Copy)
                    A(sp4(CIN[c % 2]), sm(slot(c)), ACT.Copy).then_inc(psum_free[c % 2], 1)
                    if c == 1:
                        split(l, 2)
                split(l, 3)
                act.wait_ge(ns_stored, l + 1)
                for c in range(KH):
                    act.wait_ge(tile_done, done(l, T_CS + c))
                    A(pp(Z[c]), pr(slot(c % 2)), ACT.Copy)
                    A(sp4(Z[c]), sm(slot(c % 2)), ACT.Copy).then_inc(psum_free[c % 2], 1)
                    if c == 1:
                        split(l, 4)
                split(l, 5)

                def gates(c):
                    if c:
                        act.wait_ge(scan_ready, l * 4 + c)
                    act.wait_ge(gate_done, l * 8 + (2 * c + 3))
                    for m, (row, b, v) in enumerate(((TR, B_R, V_BA), (TI, B_I, V_BX))):
                        bias = CUR[:, v + c:v + c + 1]
                        A(row[:, PADS:SB0], PS[:, b, :], ACT.Sigmoid, bias=bias)
                        A(spad(row)[:, :, PADS:SW], PS[:, B_MISC, m * NST_:(m + 1) * NST_].rearrange("p (b t) -> p b t", t=TS),
                          ACT.Sigmoid, bias=bias).then_inc(gate_read, 1)
                    act.wait_ge(gate_read, l * 8 + (2 * c + 2))
                    A(TT[:, PADS:], TR[:, PADS:], ACT.Tanh, scale=CUR[:, V_SP + c:V_SP + c + 1])
                    A(TR[:, PADS:], TR[:, PADS:], ACT.Exp, scale=CUR[:, V_NSP + c:V_NSP + c + 1]).then_inc(lru_act, 1)

                def root(c):
                    act.wait_ge(m2_ready, l * 4 + (c + 1))
                    A(TT[:, PADS:], TT[:, PADS:], ACT.Sqrt).then_inc(lru_act, 1)

                def sc_round(c):
                    act.wait_ge(psum_free[c % 2], read(l, T_BS + c))
                    A(MH[:, 4 + c], halves(HID[c % 2]), ACT.Copy).then_inc(prod_hi, 1)

                gates(0)
                root(0)
                split(l, 6)
                ada_rows(l * 3 + 2)
                gates(1)
                root(1)
                split(l, 7)
                sc_round(0)
                split(l, 8)
                gates(2)
                sc_round(1)
                root(2)
                sc_round(2)
                split(l, 9)
                gates(3)
                sc_round(3)
                root(3)
                for c in range(KH):
                    act.wait_ge(tile_done, done(l, T_GL + c))
                    if c >= 2:
                        act.wait_ge(lru_prod, l * 4 + (c - 1))
                    A(CIN[c % 2][:, PADS:PADS + TOK].rearrange("p (h n) -> p h n", h=2), slot(c % 2),
                      ACT.Gelu_apprx_tanh).then_inc(psum_free[c % 2], 1)
                    if c == 1:
                        split(l, 10)
                    act.wait_ge(lru_prod, l * 4 + (c + 1))
                    A(MH[:, c], halves(HID[c % 2]), ACT.Copy).then_inc(prod_hi, 1)
                ada_rows(l * 3 + 3)
                split(l, 11)
                act.preload_act_table(ACT.Sqrt)
                for m in range(KX):
                    square(l * 18, m)
                    if m in (1, 3, 5):
                        split(l, 12 + m // 2)
                square(l * 18, KX)
                ada_rows(l * 3 + 4)
                std(l * 2 + 2)
                split_halves(l, T_UP[0] // 2 + 1)
                act.preload_act_table(ACT.Gelu_apprx_tanh)
                norm_round(l * 2 + 2, l * 16 + 8, MOD_SH2)

                def up_quad(g, q, made, v_slot):
                    if v_slot == 0:
                        split(l, T_UP[g] // 2 + 1, q)
                    for e in range(2):
                        act.wait_ge(tile_done, l * TL + q * 4 + (T_UP[g] + e + 5))
                        A(pp(CIN[e]), pr(slot(e)), ACT.Copy)
                        A(sp4(CIN[e]), sm(slot(e)), ACT.Copy).then_inc(psum_free[e], 1)
                    split(l, T_UP[g] // 2 + 2, q)
                    for e in range(2):
                        act.wait_ge(conv_out, l * KF + q * 2 + (made + e + 1))
                        A(GE[e][:, PADS:], UC[e][:, PADS:], ACT.Gelu_apprx_tanh).then_inc(gelu_out, 1)
                    for e in range(2):
                        act.wait_ge(psum_free[e], l * PL + q * 2 + (T_UP[g] // 2 + 3))
                        A(MH[:, bass.ds(q * 2 + e, 1)].rearrange("p o h n -> p (o h) n"), halves(HID[e]), ACT.Copy)\
                            .then_inc(prod_hi, 1)

                made = 0
                for g, K in enumerate(GROUPS):
                    if g:
                        act.preload_act_table(ACT.Gelu_apprx_tanh)
                    else:
                        up_quad(0, 0, 0, 2)
                    with act.Fori(1 if g == 0 else 0, K // 2) as q:
                        up_quad(g, q, made, 0)
                    nd = T_DN[g] // 2
                    split(l, nd + 1)
                    if g < 2:
                        for n in range(nd + 2, nd + 5):
                            split(l, n)
                    else:
                        act.preload_act_table(ACT.Sqrt)
                        for m in range(KX):
                            square(l * 18 + 9, m)
                            if m in (1, 3):
                                split(l, nd + 2 + m // 2)
                            if m == 5:
                                split(l, PL)
                            if m == 4:
                                act.wait_ge(ns_rows, l + 1)
                                for i, (c0, n) in enumerate(NST):
                                    A(NSR[0:n, i, :], PS[0:n, B_MISC if i < 4 else B_R, (i % 4) * P:(i % 4 + 1) * P],
                                      ACT.Copy).then_inc(ns_read, 1)
                        square(l * 18 + 9, KX)
                        std(l * 2 + 3)
                    made += K

        @block.vector
        def _(dve):
            V = nc.vector

            class Steps:
                base, n = 0, 0

                def __call__(self, ins):
                    ins.then_inc(dve_step, 1)
                    self.n += 1
                    dve.wait_ge(dve_step, self.base + self.n)

            step = Steps()
            dve.sem_inc(lo_done, 2)
            dve.sem_inc(psum_free[0], 1)
            dve.sem_inc(psum_free[1], 1)

            def split(l, n, q=0):
                s = n % 2
                dve.wait_ge(hi_done, l * PL + q * 2 + (n + 1))
                V.tensor_tensor(WL[:, s], RAW[:, s], WH[:, s].bitcast(F32), ALU.subtract).then_inc(lo_done, 1)

            def split_half(m, l, n, part):
                s, k = n % 2, slice(0, KX // 2) if part == 0 else slice(KX // 2, KX)
                dve.wait_ge(*((hi_done, l * PL + (n + 1)) if part else (hi_half, m)))
                V.tensor_tensor(WL[:, s, k], RAW[:, s, k], WH[:, s, k].bitcast(F32), ALU.subtract)\
                    .then_inc(lo_done if part else lo_half, 1)

            def low(dst_lo, src, hi, signal):
                V.tensor_tensor(dst_lo, src, hi.bitcast(F32), ALU.subtract).then_inc(signal, 1)

            def product(row, g2, g4, src, signal):
                V.tensor_tensor(pr(halves(row)), g2, pr(src), ALU.mult)
                V.tensor_tensor(sm(halves(row)), g4, sm(src), ALU.mult).then_inc(signal, 1)

            def modulation(m, c0, bias):
                dve.wait_ge(ada_cols_done, m)
                out = MOD[:, c0:c0 + 16, :].rearrange("p (g q) j -> p g q j", g=4)
                src = PS[:, B_MISC, :].rearrange("p (q g j) -> p g q j", q=4, g=4)[:, :, :, 0:NJ]
                b = bias.rearrange("p (g q u) -> p g q u", g=4, u=1).broadcast_to([P, 4, 4, NJ])
                V.tensor_tensor(out, src, b, ALU.add).then_inc(mod_ready, 1)

            def gains(c0, v):
                step(V.tensor_scalar(GS[:], MOD[:, c0:c0 + KX, :], 1.0, None, ALU.add))
                g = CUR[:, v:v + KX].rearrange("p (k u) -> p k u", u=1).broadcast_to([P, KX, NJ])
                step(V.tensor_tensor(GS[:], GS[:], g, ALU.mult))

            def sum_square(n, m, sq=SQ):
                dve.wait_ge(sq_ready, n + (m + 1))
                if m == 0:
                    ins = V.tensor_copy(ACC, sq[0])
                else:
                    ins = V.tensor_tensor(ACC, ACC, sq[m % 2], ALU.add)
                step(ins)

            def sum_half(n, h, sq=SQ):
                dve.wait_ge(sq_ready, n)
                acc = halves(ACC)[:, h]
                V.tensor_tensor(acc, acc, halves(sq[1])[:, h], ALU.add).then_inc(acc_ready, 1)

            def rstd(m, h):
                c = 3 * h
                dve.wait_ge(std_ready, m * 2 + (h - 1))
                step(V.reciprocal(RST[:, c:c + 3], STD[:, c:c + 3]))
                V.tensor_tensor(DIAG[:, c:c + 3], IDN[:].rearrange("p (u n) -> p u n", u=1).broadcast_to([P, 3, P]),
                                RST[:, c:c + 3].rearrange("p (i u) -> p i u", u=1).broadcast_to([P, 3, P]),
                                ALU.mult).then_inc(diag_ready, 1)

            def normalise(m, n, sh, between):
                def scaled(k):
                    rs = PS[:, 6:8, 0:HALF] if k < 2 else halves(RSS)
                    V.tensor_tensor(halves(T1[k % 2]), X[:, k], rs, ALU.mult).then_inc(t1_ready, 1)
                    dve.wait_ge(t1_ready, n + (k + 1))
                dve.wait_ge(rs_done, m * 2)
                scaled(0)
                for k in range(KX + 1):
                    if k < KX:
                        f, t = sm(halves(HID[k % 2])), sm(halves(T1[k % 2]))
                        step(V.tensor_tensor(f, t, perseq(GS[:, k, 1:NJ]), ALU.mult))
                        V.tensor_tensor(f, f, perseq(MOD[:, sh + k, 1:NJ]), ALU.add).then_inc(norm_f, 1)
                    if k:
                        dve.wait_ge(norm_hi, n + k)
                        low(NL[:, k - 1], halves(HID[(k - 1) % 2]), NH[:, k - 1], norm_ready)
                    if k < KX - 1:
                        if k == 1:
                            dve.wait_ge(rs_copied, m)
                        scaled(k + 1)
                    if k == 2:
                        between()

            def residual(wait, s, xm, mod, free, signal=None):
                dve.wait_ge(tile_done, wait)
                V.scalar_tensor_tensor(out=pr(xm), in0=pr(slot(s)), scalar=mod(0, 1), in1=pr(xm),
                                       op0=ALU.mult, op1=ALU.add)
                tmp = XTMP[:, s].rearrange("p (h b t) -> p h b t", h=2, t=TS)
                V.tensor_tensor(tmp, sm(slot(s)), perseq(mod(1, NJ)), ALU.mult).then_inc(psum_free[s], 1)
                dve.wait_ge(psum_free[s], free)
                ins = V.tensor_tensor(sm(xm), sm(xm), tmp, ALU.add)
                if signal is None:
                    step(ins)
                else:
                    ins.then_inc(signal, 1)

            def last_residual(h, ready, c, free):
                dve.wait_ge(*ready)
                x = X[:, KX - 1, h]
                V.scalar_tensor_tensor(out=x[:, 0:HP], in0=PS[:, 2 + h, 0:HP], scalar=MOD[:, c, 0:1], in1=x[:, 0:HP],
                                       op0=ALU.mult, op1=ALU.add)
                tmp = XTMP[:, 1].rearrange("p (h b t) -> p h b t", h=2, t=TS)[:, h]
                gate = MOD[:, c, 1 + h * HB:1 + (h + 1) * HB].rearrange("p (b u) -> p b u", u=1).broadcast_to([P, HB, TS])
                ins = V.tensor_tensor(tmp, PS[:, 2 + h, HP:HALF].rearrange("p (b t) -> p b t", t=TS), gate, ALU.mult)
                if h == 0:
                    step(ins)
                else:
                    ins.then_inc(psum_free[1], 1)
                    dve.wait_ge(psum_free[1], free)
                xs = x[:, HP:HALF].rearrange("p (b t) -> p b t", t=TS)
                V.tensor_tensor(xs, xs, tmp, ALU.add).then_inc(x_ready, 1)

            def residual_and_norm(l, n, t, c, m):
                last_residual(0, (half_done, m - 1), c, None)
                sum_square(n, KX - 2)
                sum_half(n + KX, 0)
                last_residual(1, (tile_done, done(l, t)), c, read(l, t))
                sum_half(n + (KX + 1), 1)
                rstd(m, 0)

            def conv3(out, row, w):
                step(V.tensor_scalar(out[:, PADS:], row[:, PADS:], w(2), None, ALU.mult))
                for k in range(2):
                    ins = V.scalar_tensor_tensor(out=out[:, PADS:], in0=row[:, k + 1:PADW - 2 + k], scalar=w(k),
                                                 in1=out[:, PADS:], op0=ALU.mult, op1=ALU.add)
                    if k == 0:
                        step(ins)
                return ins

            step(V.memset(CT[:], 0.0))
            step(V.memset(STD[:], 1.0))
            dve.wait_ge(c_sig, 1)
            step(V.tensor_tensor(CT[:, :, 0], PS[:, B_MISC, 0:8], SMALL[:, 0:8], ALU.mult))
            V.tensor_tensor(CT[:, :, 1:NJ], PS[:, B_MISC, 8:72].rearrange("p (b k) -> p k b", k=KX),
                            SMALL[:, 8:72].rearrange("p (b k) -> p k b", k=KX), ALU.mult).then_inc(c_ready, 1)
            for i, h, t0, w in token_tiles():
                if i % 2 == 0:
                    dve.wait_ge(x_cols, i + 1)
                    V.tensor_copy(X[:, :, h, t0:t0 + w], turned(i)[:, :, 0:w]).then_inc(x_moved, 1)
            for k in range(KX - 1):
                sum_square(0, k, SQ0)
            for h in range(2):
                sum_half(KX, h, SQ0)
            dve.wait_ge(lam_e, 1)
            E, Zs, Z2, Q, M0 = (SMALL[:, c:c + 8] for c in (88, 96, 104, 112, 120))
            step(V.tensor_scalar(Q, E, 2.0, None, ALU.add))
            step(V.reciprocal(Q, Q))
            step(V.tensor_tensor(Zs, E, Q, ALU.mult))
            step(V.tensor_tensor(Z2, Zs, Zs, ALU.mult))
            step(V.tensor_scalar(Q, Z2, 1.0 / 17, None, ALU.mult))
            for d in (15, 13, 11, 9, 7, 5, 3):
                step(V.scalar_tensor_tensor(out=Q, in0=Q, scalar=1.0 / d, in1=Z2, op0=ALU.add, op1=ALU.mult))
            step(V.scalar_tensor_tensor(out=Q, in0=Q, scalar=1.0, in1=Zs, op0=ALU.add, op1=ALU.mult))
            for l in range(L):
                m0, q0 = M0[:, 4 * l:4 * l + 4], Q[:, 4 * l:4 * l + 4]
                step(V.tensor_scalar(m0, VEC[:, l, V_LAM:V_LAM + 4], -1.0, 0.0, ALU.mult, ALU.max))
                step(V.scalar_tensor_tensor(out=m0, in0=q0, scalar=2.0, in1=m0, op0=ALU.mult, op1=ALU.add))
                step(V.tensor_scalar(VEC[:, l, V_SP:V_SP + 4], m0, RG_C, None, ALU.mult))
                step(V.tensor_scalar(VEC[:, l, V_NSP:V_NSP + 4], m0, -RG_C, None, ALU.mult))
            rstd(1, 0)
            rstd(1, 1)
            split(0, 0)
            modulation(1, MOD_SH1, VEC[:, 0, 0:16])
            step(V.tensor_copy(CUR[:], VEC[:, 0, :]))
            dve.wait_ge(mod_ready, 1)
            gains(MOD_SC1, V_N1)
            dve.wait_ge(ada_slices, KX + 1)
            for row in Z:
                V.memset(spad(row)[:, :, 0:PADS], 0.0)
            for row in (TR, TI):
                V.memset(row[:, 0:PADS], 0.0)
                V.memset(spad(row)[:, :, 0:PADS], 0.0)
            V.memset(CIN[0][:, 0:PADS], 0.0)
            step(V.memset(CIN[1][:, 0:PADS], 0.0))
            before = step.n

            with dve.Fori(0, L) as l:
                step.base, step.n = l * DVE_STEPS + before, 0
                after = l * -1 + (L - 1)
                split_half(l * 2 + 1, l, 1, 0)
                normalise(l * 2 + 1, l * 16, MOD_SH1, lambda: split_half(l * 2 + 1, l, 1, 1))
                slc = CUR[:, V_SLC:V_SLC + 96].rearrange("p (b k c) -> p b k c", k=3, c=KH)
                nlcs = NS[:, N_LCS:N_LCS + 96].rearrange("p (b k c) -> p b k c", k=3, c=KH)
                nlcp = NS[:, N_LCP:N_LCP + 12].rearrange("p (k c) -> p k c", c=KH)
                for c in range(KH):
                    row, s = CIN[c % 2], c % 2
                    step(V.tensor_copy(spad(row)[:, :, 0:3], slc[:, :, :, c]))
                    dve.wait_ge(psum_free[s], read(l, c))
                    V.tensor_copy(nlcp[:, :, c], row[:, SB0 - 3:SB0])
                    V.tensor_copy(nlcs[:, :, :, c], spad(row)[:, :, SW - 3:SW])
                    cw = [CUR[:, V_CW + 4 * k + c:V_CW + 4 * k + c + 1] for k in range(4)]
                    out = XC[c][:, PADS:]
                    step(V.tensor_scalar(out, row[:, PADS:], cw[3], CUR[:, V_CB + c:V_CB + c + 1], ALU.mult, ALU.add))
                    for k in range(3):
                        ins = V.scalar_tensor_tensor(out=out, in0=row[:, k:PADW - 3 + k], scalar=cw[k], in1=out,
                                                     op0=ALU.mult, op1=ALU.add)
                        if k < 2:
                            step(ins)
                    ins.then_inc(xc_ready, 1)
                    if c == 0:
                        split(l, 2)
                split(l, 3)
                dve.wait_ge(ns_stored, l + 1)
                ssc = CUR[:, V_SSC:V_SSC + 64].rearrange("p (b k c) -> p b k c", k=2, c=KH)
                for c in range(KH):
                    step(V.memset(Z[c][:, 0:PADS], 0.0))
                    step(V.tensor_copy(spad(Z[c])[:, :, 1:3], ssc[:, :, :, c]))
                split(l, 4)
                split(l, 5)

                def c_times_h(c):
                    s = c % 2
                    dve.wait_ge(psum_free[s], read(l, T_CS + c))
                    dve.wait_ge(tile_done, done(l, T_HS + c))
                    V.tensor_tensor(pp(Z[c]), pp(Z[c]), pr(slot(s)), ALU.mult)
                    V.tensor_tensor(sp4(Z[c]), sp4(Z[c]), sm(slot(s)), ALU.mult).then_inc(psum_free[s], 1)
                    dve.wait_ge(psum_free[s], read(l, T_HS + c))
                    V.tensor_copy(NS[:, N_SCP:N_SCP + 8].rearrange("p (k c) -> p k c", c=KH)[:, :, c], Z[c][:, SB0 - 2:SB0])
                    V.tensor_copy(NS[:, N_SCS:N_SCS + 64].rearrange("p (b k c) -> p b k c", k=2, c=KH)[:, :, :, c],
                                  spad(Z[c])[:, :, SW - 2:SW])

                def lru_m2(c):
                    dve.wait_ge(lru_act, l * 8 + (2 * c + 1))
                    step(V.tensor_tensor(CIN[1][:, PADS:], TR[:, PADS:], TR[:, PADS:], ALU.mult))
                    V.scalar_tensor_tensor(out=TT[:, PADS:], in0=CIN[1][:, PADS:], scalar=1.0, in1=TT[:, PADS:],
                                           op0=ALU.add, op1=ALU.mult).then_inc(m2_ready, 1)
                    step(V.tensor_tensor(TI[:, PADS:], TI[:, PADS:], XC[c][:, PADS:], ALU.mult))

                def lru_scan(c):
                    dve.wait_ge(lru_act, l * 8 + (2 * c + 2))
                    step(V.tensor_tensor(TI[:, PADS:], TI[:, PADS:], TT[:, PADS:], ALU.mult))
                    step(V.memset(spad(TI)[:, :, 0:2], 0.0))
                    h0 = CUR[:, V_SH:V_SH + 32].rearrange("p (b c) -> p b c", c=KH)
                    step(V.tensor_copy(spad(TI)[:, :, 2], h0[:, :, c]))
                    step(V.memset(spad(TR)[:, :, 0:PADS], 0.0))
                    V.tensor_tensor_scan(XC[c][:, PADS:], TR[:, PADS:], TI[:, PADS:], 0.0, ALU.mult, ALU.add)\
                        .then_inc(scan_ready, 1)
                    dve.wait_ge(scan_ready, l * 4 + (c + 1))
                    V.tensor_copy(NS[:, N_HP + c:N_HP + c + 1], XC[c][:, SB0 - 1:SB0])
                    V.tensor_copy(NS[:, N_HS:N_HS + 32].rearrange("p (b c) -> p b c", c=KH)[:, :, c],
                                  spad(XC[c])[:, :, SW - 1])

                def sc_product(c):
                    s = c % 2
                    step(conv3(CIN[0], Z[c], lambda k: CUR[:, V_SW + 4 * k + c:V_SW + 4 * k + c + 1]))
                    dve.wait_ge(tile_done, done(l, T_BS + c))
                    product(HID[s], pp(CIN[0]), sp4(CIN[0]), slot(s), psum_free[s])

                def sc_low(c):
                    dve.wait_ge(prod_hi, l * 30 + (c + 1))
                    low(ML[:, 4 + c], halves(HID[c % 2]), MH[:, 4 + c], mid_ready)

                c_times_h(0)
                c_times_h(1)
                lru_m2(0)
                c_times_h(2)
                lru_scan(0)
                split(l, 6)
                c_times_h(3)
                lru_m2(1)
                lru_scan(1)
                modulation(l * 3 + 2, 16, CUR[:, 16:32])
                split(l, 7)
                sc_product(0)
                sc_low(0)
                sc_product(1)
                split(l, 8)
                lru_m2(2)
                sc_low(1)
                sc_product(2)
                lru_scan(2)
                sc_low(2)
                sc_product(3)
                split(l, 9)
                lru_m2(3)
                sc_low(3)
                lru_scan(3)
                for c in range(KH):
                    s = c % 2
                    dve.wait_ge(psum_free[s], read(l, T_GL + c))
                    gl = CIN[s][:, PADS:PADS + TOK].rearrange("p (h n) -> p h n", h=2)
                    product(HID[s], pp(XC[c]), sp4(XC[c]), gl, lru_prod)
                    if c == 1:
                        split(l, 10)
                    dve.wait_ge(prod_hi, l * 30 + (c + 5))
                    low(ML[:, c], halves(HID[s]), MH[:, c], mid_ready)
                split(l, 11)
                for m in range(KX - 1):
                    residual(done(l, T_WOUT + m), m % 2, X[:, m], lambda a_, b_, m=m: MOD[:, MOD_G1 + m, a_:b_],
                             read(l, T_WOUT + m), x_ready)
                    if m == 0:
                        modulation(l * 3 + 3, 32, CUR[:, 32:48])
                        dve.wait_ge(mod_ready, l * 3 + 3)
                        gains(MOD_SC2, V_N2)
                    else:
                        sum_square(l * 18 + 8, m - 1)
                    if m in (1, 3, 5):
                        split(l, 12 + m // 2)
                residual_and_norm(l, l * 18 + 8, T_WOUT + KX - 1, MOD_G1 + KX - 1, l * 2 + 2)
                step(V.tensor_copy(BNEXT[:], VEC[:, bass.ds(after, 1), 0:16].rearrange("p o n -> p (o n)")))
                rstd(l * 2 + 2, 1)
                split_half(l * 2 + 2, l, T_UP[0] // 2 + 1, 0)
                normalise(l * 2 + 2, l * 16 + 8, MOD_SH2, lambda: split_half(l * 2 + 2, l, T_UP[0] // 2 + 1, 1))

                ssf = CUR[:, V_SF:V_SF + 352].rearrange("p (b k m) -> p b k m", k=2, m=KF)
                nfs = NS[:, N_FS:N_FS + 352].rearrange("p (b k m) -> p b k m", k=2, m=KF)
                nfp = NS[:, N_FP:N_FP + 44].rearrange("p (k m) -> p k m", m=KF)
                def up_quad(g, q, made, v_slot):
                    if v_slot == 0:
                        split(l, T_UP[g] // 2 + 1, q)
                    for e in range(2):
                        row = CIN[e]
                        ch = bass.ds(q * 2 + (made + e), 1)
                        step(V.tensor_copy(spad(row)[:, :, 1:3], ssf[:, :, :, ch].rearrange("p b k o -> p b (k o)")))
                        dve.wait_ge(psum_free[e], l * PL + q * 2 + (T_UP[g] // 2 + 2))
                        V.tensor_copy(nfp[:, :, ch].rearrange("p k o -> p (k o)"), row[:, SB0 - 2:SB0])
                        V.tensor_copy(nfs[:, :, :, ch].rearrange("p b k o -> p b (k o)"), spad(row)[:, :, SW - 2:SW])
                        conv3(UC[e], row, lambda k: CUR[:, bass.ds(q * 2 + (V_FW + KF * k + made + e), 1)])\
                            .then_inc(conv_out, 1)
                        if e == (0 if v_slot else 1):
                            split(l, T_UP[g] // 2 + 2, q)
                    for e in range(2):
                        dve.wait_ge(tile_done, l * TL + q * 4 + (T_UP[g] + 2 + e + 5))
                        dve.wait_ge(gelu_out, l * KF + q * 2 + (made + e + 1))
                        product(HID[e], pp(GE[e]), sp4(GE[e]), slot(v_slot + e), psum_free[e])
                        dve.wait_ge(prod_hi, l * 30 + q * 2 + (8 + made + e + 1))
                        mid = bass.ds(q * 2 + e, 1)
                        low(ML[:, mid].rearrange("p o h n -> p (o h) n"), halves(HID[e]),
                            MH[:, mid].rearrange("p o h n -> p (o h) n"), mid_ready)

                made = 0
                for g, K in enumerate(GROUPS):
                    base, at, first = step.base, step.n, 0
                    if g == 0:
                        up_quad(0, 0, 0, 2)
                        first = 1
                        assert step.n == at + UP_STEPS
                    with dve.Fori(first, K // 2) as q:
                        step.base, step.n = base + at + q * UP_STEPS, 0
                        up_quad(g, q, made, 0)
                        assert step.n == UP_STEPS, step.n
                    step.base, step.n = base, at + UP_STEPS * (K // 2)
                    if g == 0:
                        modulation(l * 3 + 4, MOD_SH1, BNEXT[:])
                    nd = T_DN[g] // 2
                    if g < 2:
                        base, at = step.base, step.n
                        with dve.Fori(0, 2) as q:
                            step.base, step.n = base + at + q * 4, 0
                            for e in range(4):
                                if e % 2 == 0:
                                    split(l, nd + 1 + e // 2, q)
                                residual(l * TL + q * 4 + (T_DN[g] + e + 5), e % 2,
                                         X[:, bass.ds(q * 4 + e, 1)].rearrange("p o h n -> p (o h) n"),
                                         lambda a_, b_, e=e: MOD[:, bass.ds(q * 4 + (MOD_G2 + e), 1), a_:b_]
                                         .rearrange("p o j -> p (o j)"),
                                         l * PL + q * 2 + (T_DN[g] // 2 + e // 2 + 2))
                            assert step.n == 4
                        step.base, step.n = base, at + 8
                    else:
                        V.tensor_copy(XTMP[:, 0, 0:1], NS[:, 0:1]).then_inc(ns_ready, 1)
                        dve.wait_ge(ns_ready, l + 1)
                        split(l, nd + 1)
                        step(V.tensor_copy(CUR[:], VEC[:, bass.ds(after, 1), :].rearrange("p o n -> p (o n)")))
                        dve.wait_ge(mod_ready, l * 3 + 4)
                        gains(MOD_SC1, V_N1)
                        for m in range(KX - 1):
                            residual(done(l, T_DN[g] + m), m % 2, X[:, m], lambda a_, b_, m=m: MOD[:, MOD_G2 + m, a_:b_],
                                     read(l, T_DN[g] + m), x_ready)
                            if m:
                                sum_square(l * 18 + 17, m - 1)
                            if m in (1, 3):
                                split(l, nd + 2 + m // 2)
                            if m == 5:
                                split(l, PL)
                        residual_and_norm(l, l * 18 + 17, T_DN[g] + KX - 1, MOD_G2 + KX - 1, l * 2 + 3)
                        rstd(l * 2 + 3, 1)
                    made += K
                assert step.n == DVE_STEPS, step.n
            step.base, step.n = L * DVE_STEPS + before, 0
            dve.wait_ge(fg_in, 16)
            for i, h, t0, w in token_tiles():
                s = i % 3
                dve.wait_ge(y_cols, i + 1)
                V.scalar_tensor_tensor(out=YROW[i][0:w].rearrange("p (b n) -> p b n", b=2), in0=PS[0:w, 2 * s:2 * s + 2, :],
                                       scalar=RST[0:w, 3 * h + t0 // P:3 * h + t0 // P + 1], in1=FGB[0:w].rearrange("p (b n) -> p b n", b=2),
                                       op0=ALU.mult, op1=ALU.mult).then_inc(y_rows, 1)


UP_STEPS = 6
DVE_STEPS = 184

_OUT = ["y_prompt", "y_sample", "new_lru_h_p", "new_lru_conv_p", "new_sc_conv_p", "new_ffn_conv_p",
        "new_lru_h_s", "new_lru_conv_s", "new_sc_conv_s", "new_ffn_conv_s"]
_INS = ["x_prompt", "x_sample", "c_prompt", "c_sample", "state_lru_h", "state_lru_conv", "state_sc_conv",
        "state_ffn_conv", "w_ada", "b_ada", "norm1_g", "norm2_g", "w_in", "lru_conv_w", "lru_conv_b", "lru_wa",
        "lru_ba", "lru_wx", "lru_bx", "lru_lambda", "sc_conv_w", "w_out", "ffn_w_up", "ffn_conv_w", "ffn_w_down",
        "final_g"]


def kernel(**inputs):
    import numpy as np
    import concourse.bacc as bacc
    from concourse.bass_utils import run_bass_kernel_spmd

    nc = bacc.Bacc("TRN2", target_bir_lowering=False, num_devices=1)
    arrays, a, o = {}, {}, {}
    for name in _INS:
        arrays["in_" + name] = x = np.ascontiguousarray(inputs[name])
        a[name] = nc.dram_tensor("in_" + name, x.shape, mybir.dt.from_np(x.dtype), kind="ExternalInput").ap()
    L, DB, _, DH = inputs["state_lru_conv"].shape
    DFF = inputs["state_ffn_conv"].shape[3]
    shapes = [inputs["x_prompt"].shape, inputs["x_sample"].shape]
    for b in (1, DB):
        shapes += [(L, b, DH), (L, b, 3, DH), (L, b, 2, DH), (L, b, 2, DFF)]
    for name, shape in zip(_OUT, shapes):
        o[name] = nc.dram_tensor("out_" + name, tuple(shape), F32, kind="ExternalOutput").ap()
    hybrid_trunk_kernel(nc, a, o)
    r = run_bass_kernel_spmd(nc, [arrays], core_ids=[0])
    return tuple(r.results[0]["out_" + name] for name in _OUT)
```
